# Optimizing a Trainium2 kernel written in Bass

```python
import jax, jax.numpy as jnp
from jax import lax
import numpy as np

D_MODEL = 1024
BATCH = 1
SEQ = 512
DEPTH = 1

D_MIX = D_MODEL
ATT_HEAD_DIM = 64
ATT_HEADS = (D_MIX // 2) // ATT_HEAD_DIM
ATT_WIDTH = ATT_HEADS * ATT_HEAD_DIM
IDX_HEADS = 8
IDX_HEAD_DIM = 64
TOPK_MAX = 256
Q_BLOCK = 128
DN_HEAD_DIM = 128
DN_HEADS = (D_MIX - ATT_WIDTH) // DN_HEAD_DIM
DN_WIDTH = DN_HEADS * DN_HEAD_DIM
CONV_KERNEL = 4
CHUNK = 64
EPS = 1e-6
NEG = -1e30

SPLITS = (ATT_WIDTH, ATT_WIDTH, ATT_WIDTH, ATT_WIDTH,
          IDX_HEADS * IDX_HEAD_DIM, IDX_HEAD_DIM, IDX_HEADS,
          DN_WIDTH, DN_WIDTH, DN_WIDTH, DN_WIDTH,
          DN_HEADS, DN_HEADS)
D_IN = 4 * ATT_WIDTH + IDX_HEADS * IDX_HEAD_DIM + IDX_HEAD_DIM + IDX_HEADS + 4 * DN_WIDTH + 2 * DN_HEADS

kernel_name = "hybrid_dsa_gated_deltanet_parallel_heads"

def rms_norm(x, w):
    xf = x.astype(jnp.float32)
    y = xf * lax.rsqrt(jnp.mean(xf * xf, axis=-1, keepdims=True) + EPS)
    return (y * w.astype(jnp.float32)).astype(x.dtype)

def layer_norm_f32(x, w, b):
    xf = x.astype(jnp.float32)
    mu = jnp.mean(xf, axis=-1, keepdims=True)
    var = jnp.mean(jnp.square(xf - mu), axis=-1, keepdims=True)
    return (xf - mu) * lax.rsqrt(var + EPS) * w.astype(jnp.float32) + b.astype(jnp.float32)

def l2_norm_f32(x):
    return x * lax.rsqrt(jnp.sum(x * x, axis=-1, keepdims=True) + EPS)

def causal_depthwise_conv(x, w):
    width = w.shape[0]
    return lax.conv_general_dilated(
        x, w[:, None, :].astype(x.dtype), window_strides=(1,), padding=[(width - 1, 0)],
        dimension_numbers=("NWC", "WIO", "NWC"), feature_group_count=x.shape[-1])

def dsa_sparse_attention(q, k, v, q_idx, k_idx, w_idx):
    B, L, H, D = q.shape
    n_blk = L // Q_BLOCK
    topk = min(TOPK_MAX, L // 4)
    key_pos = jnp.arange(L)

    def blocks(t):
        return t.reshape(B, n_blk, Q_BLOCK, *t.shape[2:]).swapaxes(0, 1)

    def one_block(args):
        qb, qib, wb, blk = args
        q_pos = blk * Q_BLOCK + jnp.arange(Q_BLOCK)
        s = jnp.einsum("bqhd,bsd->bqhs", qib, k_idx)
        score = jnp.einsum("bqhs,bqh->bqs", jax.nn.relu(s), wb)
        causal = key_pos[None, :] <= q_pos[:, None]
        score = jnp.where(causal[None], score, NEG)
        _, idx = lax.top_k(score, topk)
        k_sel = jax.vmap(lambda kb, ib: kb[ib])(k, idx)
        v_sel = jax.vmap(lambda vb, ib: vb[ib])(v, idx)
        logits = jnp.einsum("bqhd,bqkhd->bhqk", qb.astype(jnp.float32),
                            k_sel.astype(jnp.float32)) * (D ** -0.5)
        valid = idx <= q_pos[None, :, None]
        logits = jnp.where(valid[:, None], logits, NEG)
        p = jax.nn.softmax(logits, axis=-1)
        o = jnp.einsum("bhqk,bqkhd->bqhd", p, v_sel.astype(jnp.float32))
        return o.astype(q.dtype)

    out = lax.map(one_block, (blocks(q), blocks(q_idx), blocks(w_idx), jnp.arange(n_blk)))
    return out.swapaxes(0, 1).reshape(B, L, H, D)

def chunk_gated_delta_rule(q, k, v, beta, g):
    B, L, H, Dk = q.shape
    Dv = v.shape[-1]
    N = L // CHUNK
    q = q * (Dk ** -0.5)

    def chunks(t):
        t = t.reshape(B, N, CHUNK, H, *t.shape[3:])
        return jnp.moveaxis(t, 3, 1)

    qc, kc, vc = chunks(q), chunks(k), chunks(v)
    bc, gc = chunks(beta), chunks(g)
    g_cum = jnp.cumsum(gc, axis=-1)
    lower = jnp.tril(jnp.ones((CHUNK, CHUNK), dtype=bool))
    strict = jnp.tril(jnp.ones((CHUNK, CHUNK), dtype=bool), -1)
    diff = g_cum[..., :, None] - g_cum[..., None, :]
    decay = jnp.exp(jnp.where(lower, diff, NEG))
    k_beta = kc * bc[..., None]
    v_beta = vc * bc[..., None]
    a_strict = jnp.where(strict, jnp.einsum("bhncd,bhnsd->bhncs", k_beta, kc) * decay, 0.0)
    m = a_strict + jnp.eye(CHUNK, dtype=a_strict.dtype)
    rhs = jnp.concatenate([v_beta, k_beta * jnp.exp(g_cum)[..., None]], axis=-1)
    sol = lax.linalg.triangular_solve(m, rhs, left_side=True, lower=True, unit_diagonal=True)
    u, w = sol[..., :Dv], sol[..., Dv:]
    intra = jnp.where(lower, jnp.einsum("bhncd,bhnsd->bhncs", qc, kc) * decay, 0.0)

    def to_scan(t):
        return jnp.moveaxis(t, 2, 0)

    def step(state, xs):
        q_i, k_i, u_i, w_i, a_i, g_i = xs
        v_new = u_i - jnp.einsum("bhcd,bhde->bhce", w_i, state)
        o_i = (jnp.einsum("bhcd,bhde->bhce", q_i * jnp.exp(g_i)[..., None], state)
               + jnp.einsum("bhcs,bhse->bhce", a_i, v_new))
        g_last = g_i[..., -1]
        state = (state * jnp.exp(g_last)[..., None, None]
                 + jnp.einsum("bhcd,bhce->bhde", k_i * jnp.exp(g_last[..., None] - g_i)[..., None], v_new))
        return state, o_i

    s0 = jnp.zeros((B, H, Dk, Dv), dtype=jnp.float32)
    _, o = lax.scan(step, s0, (to_scan(qc), to_scan(kc), to_scan(u), to_scan(w), to_scan(intra), to_scan(g_cum)))
    return jnp.transpose(o, (1, 0, 3, 2, 4)).reshape(B, L, H, Dv)

def setup_inputs(seed: int = 0) -> dict:
    key = jax.random.key(seed)
    ks = jax.random.split(key, 12)
    f32 = jnp.float32
    x = jax.random.normal(ks[0], (BATCH, SEQ, D_MODEL), f32)
    ln_w = 1.0 + 0.02 * jax.random.normal(ks[1], (DEPTH, D_MODEL), f32)
    w_in = jax.random.normal(ks[2], (DEPTH, D_MODEL, D_IN), f32) * D_MODEL ** -0.5
    attn_q_norm_w = 1.0 + 0.02 * jax.random.normal(ks[3], (DEPTH, ATT_HEAD_DIM), f32)
    attn_k_norm_w = 1.0 + 0.02 * jax.random.normal(ks[4], (DEPTH, ATT_HEAD_DIM), f32)
    idx_k_norm_w = 1.0 + 0.02 * jax.random.normal(ks[5], (DEPTH, IDX_HEAD_DIM), f32)
    idx_k_norm_b = 0.02 * jax.random.normal(ks[6], (DEPTH, IDX_HEAD_DIM), f32)
    dn_conv_w = jax.random.normal(ks[7], (DEPTH, CONV_KERNEL, 3 * DN_WIDTH), f32) * CONV_KERNEL ** -0.5
    dn_A_log = jnp.log(jax.random.uniform(ks[8], (DEPTH, DN_HEADS), f32, 1.0, 16.0))
    dt = jnp.exp(jax.random.uniform(ks[9], (DEPTH, DN_HEADS), f32, np.log(1e-3), np.log(1e-1)))
    dn_dt_bias = dt + jnp.log(-jnp.expm1(-dt))
    dn_norm_w = 1.0 + 0.02 * jax.random.normal(ks[10], (DEPTH, DN_HEAD_DIM), f32)
    w_out = jax.random.normal(ks[11], (DEPTH, D_MIX, D_MODEL), f32) * D_MIX ** -0.5
    return {"x": x, "ln_w": ln_w, "w_in": w_in, "attn_q_norm_w": attn_q_norm_w,
            "attn_k_norm_w": attn_k_norm_w, "idx_k_norm_w": idx_k_norm_w, "idx_k_norm_b": idx_k_norm_b,
            "dn_conv_w": dn_conv_w, "dn_A_log": dn_A_log, "dn_dt_bias": dn_dt_bias,
            "dn_norm_w": dn_norm_w, "w_out": w_out}

def reference(x, ln_w, w_in, attn_q_norm_w, attn_k_norm_w, idx_k_norm_w, idx_k_norm_b,
              dn_conv_w, dn_A_log, dn_dt_bias, dn_norm_w, w_out):
    B, L, _ = x.shape
    f32 = jnp.float32
    split_points = np.cumsum(np.array(SPLITS))[:-1].tolist()
    h = x
    for layer in range(DEPTH):
        hn = rms_norm(h, ln_w[layer])
        proj = hn @ w_in[layer]
        (aq, ak, av, ag, iq, ik, iw, dq, dk, dv, dz, db, da) = jnp.split(proj, split_points, axis=-1)

        q_a = rms_norm(aq.reshape(B, L, ATT_HEADS, ATT_HEAD_DIM), attn_q_norm_w[layer])
        k_a = rms_norm(ak.reshape(B, L, ATT_HEADS, ATT_HEAD_DIM), attn_k_norm_w[layer])
        v_a = av.reshape(B, L, ATT_HEADS, ATT_HEAD_DIM)
        q_i = iq.reshape(B, L, IDX_HEADS, IDX_HEAD_DIM).astype(f32)
        k_i = layer_norm_f32(ik, idx_k_norm_w[layer], idx_k_norm_b[layer])
        w_i = iw.astype(f32) * (IDX_HEADS ** -0.5) * (IDX_HEAD_DIM ** -0.5)
        o_a = dsa_sparse_attention(q_a, k_a, v_a, q_i, k_i, w_i).reshape(B, L, ATT_WIDTH)
        o_a = o_a * jax.nn.silu(ag)

        qkv = jax.nn.silu(causal_depthwise_conv(jnp.concatenate([dq, dk, dv], axis=-1), dn_conv_w[layer]))
        cq, ck, cv = jnp.split(qkv, [DN_WIDTH, 2 * DN_WIDTH], axis=-1)
        q_d = l2_norm_f32(cq.reshape(B, L, DN_HEADS, DN_HEAD_DIM).astype(f32))
        k_d = l2_norm_f32(ck.reshape(B, L, DN_HEADS, DN_HEAD_DIM).astype(f32))
        v_d = cv.reshape(B, L, DN_HEADS, DN_HEAD_DIM).astype(f32)
        beta = jax.nn.sigmoid(db.astype(f32))
        g = -jnp.exp(dn_A_log[layer].astype(f32)) * jax.nn.softplus(da.astype(f32) + dn_dt_bias[layer].astype(f32))
        o_d = chunk_gated_delta_rule(q_d, k_d, v_d, beta, g)
        o_d = rms_norm(o_d, dn_norm_w[layer]) * jax.nn.silu(dz.reshape(B, L, DN_HEADS, DN_HEAD_DIM).astype(f32))
        o_d = o_d.reshape(B, L, DN_WIDTH).astype(h.dtype)

        mix = jnp.concatenate([o_a.astype(h.dtype), o_d], axis=-1)
        h = h + mix @ w_out[layer]
    return h


_drawn_inputs = setup_inputs


def setup_inputs(seed=0):
    import zlib

    import numpy as np

    out = dict(_drawn_inputs(seed))
    spreads = {}
    factors = {'ln_w': 3.531,
     'attn_q_norm_w': 8.0,
     'attn_k_norm_w': 8.0,
     'idx_k_norm_w': 8.0,
     'idx_k_norm_b': 8.0,
     'dn_norm_w': 18.078}
    for name, (base, spread) in spreads.items():
        noise = np.random.default_rng([zlib.crc32(name.encode()), seed]).standard_normal(out[name].shape)
        drawn = base * np.exp(spread * noise) if base else spread * noise
        out[name] = __import__('jax').numpy.asarray(drawn.astype(out[name].dtype))
    for name, factor in factors.items():
        out[name] = (out[name] * factor).astype(out[name].dtype)
    return out
```

```python
from contextlib import ExitStack

import numpy as np

import concourse.bass as bass
from concourse import mybir

F32 = mybir.dt.float32
F32R = mybir.dt.float32r
BF16 = mybir.dt.bfloat16
U8 = mybir.dt.uint8
ALU = mybir.AluOpType
ACT = mybir.ActivationFunctionType
AX = mybir.AxisListType

P = 128
SEQ = 512
D = 1024
NT = SEQ // P
KT = D // P
AH, AD = 8, 64
DH, DD = 4, 128
TOPK = min(256, SEQ // 4)
TAPS = 4
EPS = 1e-6
NEG = -1e30
TAKEN = -3e38
LEVELS = 7
GW = 512

C_AQ, C_AK, C_AV, C_AG, C_IQ, C_IK = 0, 512, 1024, 1536, 2048, 2560
C_DQ, C_DK, C_DV, C_DZ, C_DB = 2632, 3144, 3656, 4168, 4680
MISC = 80

GROUPS = [
    ("misc", "B", C_IK, SEQ), ("iq", "B", C_IQ, SEQ - P), ("ak", "A", C_AK, GW), ("aq", "A", C_AQ, GW),
    ("av", "A", C_AV, GW), ("ag", "A", C_AG, GW), ("dk", "B", C_DK, SEQ), ("dq", "B", C_DQ, SEQ),
    ("dv", "B", C_DV, SEQ), ("dz", "A", C_DZ, GW), ("out0", "A", 0, GW), ("out1", "A", GW, GW),
]
GROUP = {g[0]: g for g in GROUPS}
UNITS = [("misc", tuple(range(KT)))] + [(g[0], (k, k + 1)) for g in GROUPS[1:] for k in range(0, KT, 2)]
RAW_RING, SPLIT_RING, AHEAD = 4, 3, 2

R_CONV, R_WQ, R_WK, R_IW, R_IB, ROWS = 0, 48, 49, 50, 51, 52


def tiles(name):
    return 1 if name == "misc" else 4


def make_plan():
    plan = [("ln_cols",)] + [("xT", k) for k in range(KT)]

    def unit(name, n):
        plan.append(("main", UNITS.index((name, tuple(range(KT)) if name == "misc" else (2 * n, 2 * n + 1)))))
        if n == 3 or name == "misc":
            plan.append(("evac", name))

    unit("misc", 0)
    plan.append(("cols",))
    unit("iq", 0)
    plan.extend([("miscT",), ("gates",)])
    for n in range(1, 4):
        unit("iq", n)
    plan.extend([("kiT",), ("gcum",)])
    idx = [("idx", qb, h) for qb in range(1, NT) for h in range(AH)]
    for n in range(4):
        unit("ak", n)
        for s in idx[6 * n:6 * n + 6]:
            plan.append(s)
            if s[2] == AH - 1:
                plan.append(("causal", s[1]))
    plan.append(("norm", "ak"))
    for n in range(4):
        unit("aq", n)
        plan.append(("topk", 1, n))
        if n == 1:
            plan.append(("scale", "ak"))
        if n == 2:
            plan.extend([("kT", j) for j in range(4)])
    plan.append(("norm", "aq"))
    for n in range(4):
        unit("av", n)
        plan.append(("topk", 2, n))
        if n == 1:
            plan.append(("scale", "aq"))
        if n == 2:
            plan.extend([("qT", j) for j in range(4)])
    att = []
    n_att = NT * AH
    for n in range(n_att + 3):
        if n < n_att:
            att.append([("qk", n)])
        else:
            att.append([])
        if 2 <= n < n_att + 2:
            att[-1].append(("pt", n - 2))
        if n >= 3:
            att[-1].append(("av", n - 3))
            if (n - 3) % AH == AH - 1:
                att[-1].append(("omix", (n - 3) // AH))
    at = 0

    def attend(n):
        nonlocal at
        for here in att[at:at + n]:
            plan.extend(here)
        at += n

    for n in range(4):
        unit("ag", n)
        plan.append(("topk", 3, n))
        attend(2)
    for g, before in (("dk", None), ("dq", "dk"), ("dv", "dq")):
        for n in range(4):
            unit(g, n)
            if before:
                plan.append(("conv", before, n))
            attend(2 if n == 0 else 3)
        if before:
            plan.append(("silu", before))
    attend(len(att))
    unit("dz", 0)
    plan.extend([("dec", 0), ("dec", 1), ("conv", "dv", 0), ("conv", "dv", 1)])
    unit("dz", 1)
    plan.extend([("dec", 2), ("decT", 0), ("conv", "dv", 2), ("conv", "dv", 3), ("silu", "dv")])
    unit("dz", 2)
    plan.extend([("dec", 3), ("decT", 1), ("decT", 2), ("dA", 0)])
    unit("dz", 3)
    plan.extend([("decT", 3), ("allbanks",)])
    plan.extend([("dA", 1), ("dB", 0), ("dA", 2), ("dC", 0), ("dB", 1), ("dA", 3), ("ones", 0), ("ones", 1), ("dC", 1), ("dB", 2)])
    mix = {1: ("dC", 2), 2: ("dB", 3), 3: ("dC", 3)}
    for l in range(LEVELS):
        plan.extend([("Z", c, l) for c in (0, 1)])
        if l + 2 < LEVELS:
            plan.append(("ones", l + 2))
        plan.extend([("TU", c, l) for c in (0, 1)])
        if l in mix:
            plan.append(mix[l])
    plan.extend([("uw", c) for c in (0, 1)])
    mix = {0: ("ws", 0), 1: ("kv", 0), 2: ("o", 0), 3: ("ws", 1), 4: ("kv", 1), 5: ("o", 1)}
    for l in range(LEVELS):
        plan.extend([("Z", c, l) for c in (2, 3)])
        if l in mix:
            plan.append(mix[l])
        plan.extend([("TU", c, l) for c in (2, 3)])
        if l in (2, 5):
            plan.append(("onorm", l // 4))
    plan.extend([("uw", 2), ("uw", 3), ("reload",), ("ws", 2), ("mixT", 0), ("mixT", 1), ("kv", 2),
                 ("o", 2), ("mixT", 2), ("mixT", 3), ("ws", 3), ("onorm", 2)])
    unit("out0", 0)
    plan.append(("o", 3))
    plan.append(("onorm", 3))
    unit("out0", 1)
    plan.extend([("mixT", k) for k in range(4, 8)])
    for n in (2, 3):
        unit("out0", n)
    for n in range(4):
        unit("out1", n)
    return plan


def assign_banks(plan):
    use, count = {}, [0] * 8
    ring, turn = [4, 5, 6, 7], 0

    def take(key, bank=None):
        nonlocal turn
        if bank is None:
            bank = ring[turn % len(ring)]
            turn += 1
        use[key] = (bank, count[bank])
        count[bank] += 1

    for s in plan:
        kind = s[0]
        if kind == "main":
            name, ks = UNITS[s[1]]
            if ks[0] == 0:
                for j in range(tiles(name)):
                    take((name, j), j)
                if name == "out0":
                    ring = [4, 5, 6, 7]
        elif kind == "allbanks":
            ring = list(range(8))
        elif kind == "qk":
            if s[1] == 0:
                ring = [4, 5, 6]
            take(s)
        elif kind in ("cols", "ln_cols", "xT", "miscT", "kiT", "gcum", "idx", "kT", "qT", "pt", "mixT", "o", "Z", "decT"):
            take(s)
        elif kind == "av":
            if s[1] % AH == 0:
                take(("O", s[1] // AH), 7)
        elif kind == "dec":
            if s[1] == 0:
                ring = [4, 5, 6, 7]
            take(s)
        elif kind == "dA":
            for x in "kqv":
                take((x, s[1]))
        elif kind == "dB":
            for x in ("knT", "qnT", "qeT"):
                take((x, s[1]))
        elif kind == "dC":
            for b in range(2):
                take(("kk", s[1], b))
        elif kind == "TU":
            _, c, l = s
            if l == LEVELS - 2:
                take(("T", c, l))
            if l > 0:
                take(("U", c, l))
        elif kind == "uw":
            take(("u", s[1]))
            take(("w", s[1]))
        elif kind == "ws" and s[1] > 0:
            take(s)
        elif kind == "kv" and s[1] < NT - 1:
            take(s)
    return use


def build(nc, x, ln_w, w_in, wq_n, wk_n, wi_n, bi_n, conv_w, a_log, dt_b, dn_w, w_out, c_f32, out):
    plan = make_plan()
    use = assign_banks(plan)
    kinds = {}
    nth = {}
    for s in plan:
        nth[s] = kinds.get(s[0], 0)
        kinds[s[0]] = nth[s] + 1
    norm_at, norm_no, at = {}, {}, 0
    for key, w in ([(("x", t), 1) for t in range(NT)] + [(("ik",), NT), (("ak",), NT * AH), (("aq",), NT * AH)]
                   + [(("dqk", c), 2 * DH) for c in range(NT)] + [(("onorm", c), DH) for c in range(NT)]):
        norm_at[key], norm_no[key] = (at, at + w), len(norm_no)
        at += w
    norm_cols = at

    with ExitStack() as ctx:
        def sb(name, shape, dt=F32):
            return ctx.enter_context(nc.sbuf_tensor(name, shape, dt))

        def sem(name):
            return ctx.enter_context(nc.semaphore(name))

        bank = [ctx.enter_context(nc.psum_tensor(f"bank{i}", [P, 512], F32)) for i in range(8)]

        w_raw = sb("w_raw", [P, RAW_RING, 2 * GW])
        w_hi = sb("w_hi", [P, SPLIT_RING, 2 * GW], F32R)
        w_lo = sb("w_lo", [P, SPLIT_RING, 2 * GW], F32R)
        in_hi = sb("in_hi", [P, KT, SEQ], F32R)
        in_lo = sb("in_lo", [P, KT, SEQ], F32R)
        gate = sb("gate", [P, NT, D])
        arena1 = sb("arena1", [P, 14 * 512])
        arena2 = sb("arena2", [P, 20480])
        consts = sb("consts", [P, 2 * P])
        ident, tri = consts[:, 0:P], consts[:, P:2 * P]
        level_mask = sb("level_mask", [P, LEVELS, P], U8)
        cbf = sb("cbf", [P, 2 * P], BF16)
        ident_bf, keep_lower = cbf[:, 0:P], cbf[:, P:2 * P]
        ones = sb("ones", [P, P])
        rows = sb("rows", [ROWS, P])
        ln_rows = sb("ln_rows", [KT, P])
        ln_cols = sb("ln_cols", [P, KT])
        cols = sb("cols", [P, ROWS])
        dnw = sb("dnw", [P, DD])
        small = sb("small", [P, 640])
        var = sb("var", [P, norm_cols])
        rstd = sb("rstd", [P, norm_cols])
        half = sb("half", [P, 32])
        misc = sb("misc", [P, NT, MISC])

        x_sb = arena1[:, 0:4096].rearrange("p (t d) -> p t d", t=NT)
        conv_out = arena1[:, 0:6144].rearrange("p (n t) -> p n t", n=12)
        zc = arena1[:, :].rearrange("p (b l n) -> p b l n", b=2, l=LEVELS)

        mask_words = gate[:, 0:2, :].rearrange("p t d -> p (t d)")[:, 0:(LEVELS + 2) * P]

        spot = [0]

        def part(words):
            spot[0] += words
            return arena2[:, spot[0] - words:spot[0]]

        iqT = part(4 * 384).rearrange("p (n t) -> p n t", n=4)
        kiT = part(512)
        qk_raw = part(2048).rearrange("p (t n) -> p t n", t=NT)
        qT = part(2048).rearrange("p (j t) -> p j t", j=4)
        kT = part(2048).rearrange("p (j t) -> p j t", j=4)
        v_sb = part(2048).rearrange("p (t n) -> p t n", t=NT)
        score = part(4 * 512).rearrange("p (q s) -> p q s", q=NT)
        masked = part(2 * 512).rearrange("p (b s) -> p b s", b=2)
        prob = part(2 * 512).rearrange("p (b s) -> p b s", b=2)
        relu = prob
        probT = part(2 * 512).rearrange("p (b s) -> p b s", b=2)
        att_out = part(128 + 384)
        attention_words = spot[0]
        miscT = prob[0:MISC, :, :].rearrange("p b s -> p (b s)")[:, 0:SEQ]
        conv_in = arena2[:, attention_words:attention_words + 4 * (SEQ + 3)].rearrange("p (j t) -> p j t", j=4)
        junk = arena2[:, 2048:2048 + D]

        spot[0] = 0
        k_dec, k_bg, v_b, qeT, a_neg, intraT = (
            part(2048).rearrange("p (c h n) -> p c h n", c=NT, h=DH) for _ in range(6))
        q_n, k_n, q_e = (part(512).rearrange("p (h n) -> p h n", h=DH) for _ in range(3))
        kqT = part(1024).rearrange("p (h x n) -> p h x n", h=DH, x=2)
        spot[0] = max(spot[0], attention_words)
        inv_u, inv_t = (part(1024).rearrange("p (b h n) -> p b h n", b=2, h=DH) for _ in range(2))
        state, v_new = (part(1024).rearrange("p (b h n) -> p b h n", b=2, h=DH) for _ in range(2))
        o_tmp = part(512)
        sq = o_tmp
        assert spot[0] <= 20480 and attention_words + 4 * (SEQ + 3) <= spot[0] - 512

        sm = [0]

        def tiny(n):
            sm[0] += n
            assert sm[0] <= 640
            return small[:, sm[0] - n:sm[0]]

        ss_x = tiny(NT)
        w_i = tiny(NT * AH).rearrange("p (t h) -> p t h", t=NT)
        mu, mu_s, ss_ik = tiny(NT), tiny(NT), tiny(NT)
        ss_att = tiny(NT * AH).rearrange("p (t h) -> p t h", t=NT)
        dt_bc, alog_bc, exp_alog = tiny(DH), tiny(DH), tiny(DH)
        y_dt, nab, e_nab, ln_sp, soft, e_b, beta, nbeta, g = (
            tiny(NT * DH).rearrange("p (t h) -> p t h", t=NT) for _ in range(9))
        gc2 = tiny(2 * NT * DH)
        gc, g_last = gc2[:, 0:NT * DH], gc2[:, NT * DH:]
        e_g, e_last, diff, e_diff, b_eg = (tiny(NT * DH) for _ in range(5))
        top8 = tiny(8)
        mx, nmx, p_sum = tiny(NT * AH), tiny(NT * AH), tiny(NT * AH)
        r_sum = tiny(AH)
        ss_d, r_q = tiny(2 * DH), tiny(DH)
        ik_c = arena2[:, 0:NT * AD].rearrange("p (t d) -> p t d", t=NT)
        ik_sq = arena2[:, 256:256 + NT * AD].rearrange("p (t d) -> p t d", t=NT)
        ik_n = arena2[:, 2048:2048 + NT * P].rearrange("p (t d) -> p t d", t=NT)

        bank_full = [sem(f"bank_full{i}") for i in range(8)]
        bank_free = [sem(f"bank_free{i}") for i in range(8)]
        raw_loaded = [sem(f"raw_loaded{i}") for i in range(RAW_RING)]
        x_loaded = [sem(f"x_loaded{t}") for t in range(NT)]
        const_loaded = sem("const_loaded")
        ln_loaded = sem("ln_loaded")
        masks_cast = sem("masks_cast")
        rows_loaded, par_loaded, masks_loaded = sem("rows_loaded"), sem("par_loaded"), sem("masks_loaded")
        x_again = sem("x_again")
        stored = sem("stored")
        hi_ready, lo_ready, w_used = sem("hi_ready"), sem("lo_ready"), sem("w_used")
        in_hi_ready = sem("in_hi_ready")
        pool_const = sem("pool_const")
        x_squared, x_normed = sem("x_squared"), sem("x_normed")
        var_ready, rstd_ready = sem("var_ready"), sem("rstd_ready")
        vec = sem("vec")
        act_own = sem("act_own")
        ik_ready, gate_in, gate_exp, g_ready = sem("ik_ready"), sem("gate_in"), sem("gate_exp"), sem("g_ready")
        gcum_ready, gcum_exp, gcum_done = sem("gcum_ready"), sem("gcum_exp"), sem("gcum_done")
        idx_added, causal_done, kept_ready = sem("idx_added"), sem("causal_done"), sem("kept_ready")
        qk_squared, qk_summed, qk_normed = sem("qk_squared"), sem("qk_summed"), sem("qk_normed")
        nmx_ready, exp_done, av_done, att_mixed = sem("nmx_ready"), sem("exp_done"), sem("av_done"), sem("att_mixed")
        conv_done, conv_silu = sem("conv_done"), sem("conv_silu")
        d_squared, d_summed, d_scaled = sem("d_squared"), sem("d_summed"), sem("d_scaled")
        dz_scaled, dec_ready, kk_done = sem("dz_scaled"), sem("dec_ready"), sem("kk_done")
        t_ready = sem("t_ready")
        zc_ones_v, zc_ones_a = sem("zc_ones_v"), sem("zc_ones_a")
        o_squared, o_summed, delta_mixed = sem("o_squared"), sem("o_summed"), sem("delta_mixed")

        def wait_full(eng, key):
            b, before = use[key]
            eng.wait_ge(bank_full[b], before + 1)

        def wait_out(eng, key):
            b, before = use[key]
            eng.wait_ge(bank_free[b], before + 1)

        def wait_bank(eng, key):
            b, before = use[key]
            if before:
                eng.wait_ge(bank_free[b], before)

        def full(key):
            return bank_full[use[key][0]]

        def free(key):
            return bank_free[use[key][0]]

        def at_bank(key):
            return bank[use[key][0]]

        def heads(ap):
            return ap.rearrange("p (h n) -> p h n", h=DH)

        def over(ap, n):
            return ap.unsqueeze(2).to_broadcast([P, ap.shape[1], n])

        def last_unit(u):
            return u == len(UNITS) - 1 or UNITS[u + 1][0] != UNITS[u][0]

        def wait_unit_used(eng, u):
            if last_unit(u):
                wait_full(eng, (UNITS[u][0], tiles(UNITS[u][0]) - 1))
            else:
                eng.wait_ge(w_used, sum(not last_unit(i) for i in range(u + 1)))

        def unit_width(u):
            return KT * MISC if UNITS[u][0] == "misc" else 2 * GW

        def wait_av(eng, i):
            if i % AH == AH - 1:
                wait_full(eng, ("O", i // AH))
            else:
                eng.wait_ge(av_done, i + 1 - (i + 1) // AH)

        def wait_t(eng, c, l):
            if l < LEVELS - 2:
                eng.wait_ge(t_ready, (c // 2 * (LEVELS - 2) + l) * 2 + c % 2 + 1)
            else:
                wait_out(eng, ("T", c, l))

        block = ctx.enter_context(nc.Block())

        @block.sync
        def _(sp):
            xs = x.rearrange("b (t p) d -> p (b t) d", p=P)
            for t in range(NT):
                sp.dma_start(x_sb[:, t, :], xs[:, t, :]).then_inc(x_loaded[t], 16)
                if t == 0:
                    sp.dma_start(ln_rows[:, :], ln_w.rearrange("a (k p) -> (a k) p", p=P)).then_inc(ln_loaded, 16)
                if t == 1:
                    sp.dma_start(consts[:, :], c_f32[:, 0:2 * P]).then_inc(const_loaded, 16)
            for u, (name, ks) in enumerate(UNITS):
                r = u % RAW_RING
                if u >= RAW_RING:
                    sp.wait_ge(hi_ready, u - RAW_RING + 1)
                    sp.wait_ge(lo_ready, u - RAW_RING + 1)
                if name == "misc":
                    dst = w_raw[:, r, 0:KT * MISC].rearrange("p (k n) -> p k n", k=KT)
                    src = w_in.rearrange("a (k p) n -> p (a k) n", p=P)
                    sp.dma_start(dst[:, :, 0:72], src[:, :, C_IK:C_IK + 72]).then_inc(raw_loaded[r], 16)
                    sp.dma_start(dst[:, :, 72:80], src[:, :, C_DB:C_DB + 8]).then_inc(raw_loaded[r], 16)
                else:
                    c0 = GROUP[name][2]
                    w = w_out if name[:3] == "out" else w_in
                    src = w.rearrange("a (k p) n -> p (a k) n", p=P)[:, ks[0]:ks[1] + 1, c0:c0 + GW]
                    sp.dma_start(w_raw[:, r, :].rearrange("p (k n) -> p k n", k=2), src).then_inc(raw_loaded[r], 16)
                if u == RAW_RING - 1:
                    sp.dma_start(mask_words, c_f32[:, 2 * P:]).then_inc(masks_loaded, 16)
            wait_full(sp, ("U", NT - 1, LEVELS - 1))
            for t in range(NT):
                sp.dma_start(x_sb[:, t, :], xs[:, t, :]).then_inc(x_again, 16)
            os_ = out.rearrange("b (t p) d -> p (b t) d", p=P)
            for n in range(2):
                for t in range(NT):
                    wait_out(sp, (f"out{n}", t))
                    sp.dma_start(os_[:, t, n * GW:(n + 1) * GW], x_sb[:, t, n * GW:(n + 1) * GW]).then_inc(stored, 16)
            sp.wait_ge(stored, 16 * 2 * NT)

        @block.tensor
        def _(pe):
            def transposes(key, srcs):
                wait_bank(pe, key)
                for i, s in enumerate(srcs):
                    ins = nc.tensor.transpose(at_bank(key)[:, i * P:(i + 1) * P], s, ident)
                ins.then_inc(full(key), 1)

            def main(u):
                name, ks = UNITS[u]
                _, layout, _, width = GROUP[name]
                slot = u % SPLIT_RING
                n = MISC if name == "misc" else GW
                hi = w_hi[:, slot, 0:len(ks) * n].rearrange("p (k n) -> p k n", k=len(ks))
                lo = w_lo[:, slot, 0:len(ks) * n].rearrange("p (k n) -> p k n", k=len(ks))
                pe.wait_ge(hi_ready, u + 1)
                pe.wait_ge(lo_ready, u + 1)
                for i, k in enumerate(ks):
                    if name == "misc":
                        wait_out(pe, ("xT", k))
                    if name == "out0":
                        wait_out(pe, ("mixT", k))
                    for j in range(tiles(name)):
                        if k == 0:
                            wait_bank(pe, (name, j))
                        dst = at_bank((name, j))[0:min(n, P), 0:width]
                        if layout == "A":
                            xh, xl = in_hi[:, k, j * P:(j + 1) * P], in_lo[:, k, j * P:(j + 1) * P]
                            pairs = ((xh, hi[:, i, :]), (xh, lo[:, i, :]), (xl, hi[:, i, :]))
                        else:
                            wh, wl = (x_[:, i, j * P:j * P + min(n, P)] for x_ in (hi, lo))
                            xh, xl = in_hi[:, k, SEQ - width:], in_lo[:, k, SEQ - width:]
                            pairs = ((wh, xh), (wh, xl), (wl, xh))
                        for m, (a, b) in enumerate(pairs):
                            ins = nc.tensor.matmul(dst, a, b, start=(k == 0 and m == 0), stop=(k == KT - 1 and m == 2))
                        if k == KT - 1:
                            ins.then_inc(full((name, j)), 1)
                if not last_unit(u):
                    ins.then_inc(w_used, 1)

            pe.wait_ge(const_loaded, 16)
            for s in plan:
                kind, a = s[0], s[1:]
                if kind == "ln_cols":
                    pe.wait_ge(ln_loaded, 16)
                    wait_bank(pe, s)
                    nc.tensor.transpose(at_bank(s)[:, 0:KT], ln_rows[:, :], ident[0:KT, 0:KT]).then_inc(full(s), 1)
                elif kind == "cols":
                    pe.wait_ge(rows_loaded, 16 * 5)
                    wait_bank(pe, s)
                    nc.tensor.transpose(at_bank(s)[:, 0:ROWS], rows[:, :], ident[0:ROWS, 0:ROWS]).then_inc(full(s), 1)
                elif kind == "xT":
                    if a[0] == 0:
                        pe.wait_ge(x_normed, NT)
                    transposes(s, [x_sb[:, t, a[0] * P:(a[0] + 1) * P] for t in range(NT)])
                elif kind == "main":
                    main(a[0])
                elif kind == "miscT":
                    wait_out(pe, ("misc", 0))
                    wait_bank(pe, s)
                    for t in range(NT):
                        ins = nc.tensor.transpose(at_bank(s)[:, t * MISC:(t + 1) * MISC],
                                                  miscT[:, t * P:(t + 1) * P], ident[0:MISC, 0:MISC])
                    ins.then_inc(full(s), 1)
                elif kind == "kiT":
                    pe.wait_ge(ik_ready, 2)
                    transposes(s, [ik_n[:, t, :] for t in range(NT)])
                elif kind == "gcum":
                    pe.wait_ge(g_ready, 1)
                    pe.wait_ge(pool_const, 2)
                    wait_bank(pe, s)
                    g16 = g.rearrange("p t h -> p (t h)")
                    nc.tensor.matmul(at_bank(s)[:, 0:16], tri, g16, start=True, stop=True)
                    nc.tensor.matmul(at_bank(s)[:, 16:32], ones[:, :], g16, start=True, stop=True).then_inc(full(s), 1)
                elif kind == "idx":
                    qb, h = a
                    wait_out(pe, ("iq", h // 2))
                    if nth[s] == 0:
                        wait_out(pe, ("kiT",))
                    wait_bank(pe, s)
                    r = slice((h % 2) * AD, (h % 2) * AD + AD)
                    n = (qb + 1) * P
                    nc.tensor.matmul(at_bank(s)[:, 0:n], iqT[r, h // 2, (qb - 1) * P:qb * P], kiT[r, 0:n],
                                     start=True, stop=True).then_inc(full(s), 1)
                elif kind in ("kT", "qT"):
                    if a[0] == 0:
                        pe.wait_ge(qk_normed, NT if kind == "kT" else 2 * NT)
                    transposes(s, [qk_raw[:, t, a[0] * P:(a[0] + 1) * P] for t in range(NT)])
                elif kind == "qk":
                    qb, h = divmod(a[0], AH)
                    wait_out(pe, ("qT", h // 2))
                    wait_out(pe, ("kT", h // 2))
                    wait_bank(pe, s)
                    r = slice((h % 2) * AD, (h % 2) * AD + AD)
                    n = (qb + 1) * P
                    nc.tensor.matmul(at_bank(s)[:, 0:n], qT[r, h // 2, qb * P:(qb + 1) * P], kT[r, h // 2, 0:n],
                                     start=True, stop=True).then_inc(full(s), 1)
                elif kind == "pt":
                    i = a[0]
                    pe.wait_ge(exp_done, i + 1)
                    transposes(s, [prob[:, i % 2, j * P:(j + 1) * P] for j in range(i // AH + 1)])
                elif kind == "av":
                    i = a[0]
                    qb, h = divmod(i, AH)
                    if h == 0:
                        wait_bank(pe, ("O", qb))
                        wait_out(pe, ("av", qb))
                    wait_out(pe, ("pt", i))
                    for j in range(qb + 1):
                        ins = nc.tensor.matmul(bank[7][:, h * AD:(h + 1) * AD], probT[:, i % 2, j * P:(j + 1) * P],
                                               v_sb[:, j, h * AD:(h + 1) * AD], start=(j == 0), stop=(j == qb))
                    ins.then_inc(full(("O", qb)) if h == AH - 1 else av_done, 1)
                elif kind == "dA":
                    c = a[0]
                    for n, (x_, first) in enumerate((("k", 0), ("q", 4), ("v", 8))):
                        pe.wait_ge(conv_silu, 4 * (n + 1))
                        transposes((x_, c), [conv_out[:, first + h, c * P:(c + 1) * P] for h in range(DH)])
                elif kind == "dB":
                    c = a[0]
                    wait_out(pe, ("k", c))
                    transposes(("knT", c), [k_n[:, h, :] for h in range(DH)])
                    wait_out(pe, ("q", c))
                    transposes(("qnT", c), [q_n[:, h, :] for h in range(DH)])
                    pe.wait_ge(d_scaled, 3 * c + 1)
                    transposes(("qeT", c), [q_e[:, h, :] for h in range(DH)])
                elif kind == "dec":
                    c = a[0]
                    if c == 0:
                        pe.wait_ge(masks_cast, 2)
                    wait_bank(pe, s)
                    nc.tensor.matmul(heads(at_bank(s)[:, :]), ident_bf, keep_lower.unsqueeze(1).to_broadcast([P, DH, P]),
                                     start=True, stop=False, skip_group_check=True)
                    for h in range(DH):
                        ins = nc.tensor.matmul(at_bank(s)[:, h * P:(h + 1) * P], g[:, c, h:h + 1].to_broadcast([P, P]),
                                               tri, start=False, stop=(h == DH - 1), skip_group_check=True)
                    ins.then_inc(full(s), 1)
                elif kind == "decT":
                    wait_out(pe, ("dec", a[0]))
                    transposes(s, [a_neg[:, a[0], h, :] for h in range(DH)])
                elif kind == "dC":
                    c = a[0]
                    wait_out(pe, ("knT", c))
                    wait_out(pe, ("qnT", c))
                    for b in range(2):
                        key = ("kk", c, b)
                        wait_bank(pe, key)
                        for i in range(2):
                            h = 2 * b + i
                            ins = nc.tensor.matmul(at_bank(key)[:, i * 256:(i + 1) * 256], kqT[:, h, 0, :],
                                                   kqT[:, h, :, :].rearrange("p x n -> p (x n)"), start=True, stop=True)
                        ins.then_inc(full(key), 1)
                elif kind == "Z":
                    c, l = a
                    if l == 0:
                        pe.wait_ge(kk_done, 2 * c + 2)
                        transposes(s, [a_neg[:, c, h, :] for h in range(DH)])
                    else:
                        if l > 1:
                            wait_out(pe, ("U", c, l - 1))
                        wait_bank(pe, s)
                        for h in range(DH):
                            u_h = heads(zc[:, c % 2, 0, :])[:, h, :] if l == 1 else inv_u[:, c % 2, h, :]
                            ins = nc.tensor.matmul(at_bank(s)[:, h * P:(h + 1) * P], a_neg[:, c, h, :], u_h,
                                                   start=True, stop=True)
                        ins.then_inc(full(s), 1)
                elif kind == "TU":
                    c, l = a
                    z = heads(zc[:, c % 2, l, :])
                    wait_out(pe, ("Z", c, l))
                    if l:
                        wait_t(pe, c, l - 1)
                        for x_ in ("T", "U"):
                            key = (x_, c, l)
                            if key not in use:
                                continue
                            wait_bank(pe, key)
                            for h in range(DH):
                                lhs, rhs = z[:, h, :], inv_t[:, c % 2, h, :]
                                if x_ == "U":
                                    lhs, rhs = rhs, lhs
                                ins = nc.tensor.matmul(at_bank(key)[:, h * P:(h + 1) * P], lhs, rhs, start=True,
                                                       stop=True)
                            ins.then_inc(full(key), 1)
                elif kind == "uw":
                    c = a[0]
                    wait_out(pe, ("U", c, LEVELS - 1))
                    pe.wait_ge(d_scaled, 3 * c + 3)
                    for key in (("u", c), ("w", c)):
                        wait_bank(pe, key)
                        for h in range(DH):
                            u_h = inv_u[:, c % 2, h, :]
                            lhs, rhs = (u_h, v_b[:, c, h, :]) if key[0] == "u" else (k_bg[:, c, h, :], u_h)
                            ins = nc.tensor.matmul(at_bank(key)[:, h * P:(h + 1) * P], lhs, rhs, start=True, stop=True)
                        ins.then_inc(full(key), 1)
                elif kind == "ws" and a[0] > 0:
                    c = a[0]
                    wait_out(pe, ("w", c))
                    wait_out(pe, ("kv", c - 1))
                    wait_bank(pe, s)
                    for h in range(DH):
                        ins = nc.tensor.matmul(at_bank(s)[:, h * P:(h + 1) * P], k_bg[:, c, h, :], state[:, c % 2, h, :],
                                               start=True, stop=True)
                    ins.then_inc(full(s), 1)
                elif kind == "kv" and a[0] < NT - 1:
                    c = a[0]
                    wait_out(pe, ("ws", c) if c else ("u", 0))
                    wait_bank(pe, s)
                    for h in range(DH):
                        vn = v_new[:, c % 2, h, :] if c else v_b[:, 0, h, :]
                        ins = nc.tensor.matmul(at_bank(s)[:, h * P:(h + 1) * P], k_dec[:, c, h, :], vn, start=True,
                                               stop=True)
                    ins.then_inc(full(s), 1)
                elif kind == "o":
                    c = a[0]
                    if c == NT - 1:
                        wait_out(pe, ("ws", c))
                    wait_out(pe, ("qeT", c))
                    wait_bank(pe, s)
                    for h in range(DH):
                        dst = at_bank(s)[:, h * P:(h + 1) * P]
                        if c:
                            nc.tensor.matmul(dst, qeT[:, c, h, :], state[:, c % 2, h, :], start=True, stop=False)
                        vn = v_new[:, c % 2, h, :] if c else v_b[:, 0, h, :]
                        ins = nc.tensor.matmul(dst, intraT[:, c, h, :], vn, start=(c == 0), stop=True)
                    ins.then_inc(full(s), 1)
                elif kind == "mixT":
                    k = a[0]
                    if k == 0:
                        pe.wait_ge(att_mixed, NT)
                    if k == 4:
                        pe.wait_ge(delta_mixed, NT)
                    transposes(s, [gate[:, t, k * P:(k + 1) * P] for t in range(NT)])

        @block.scalar
        def _(act):
            own = [0]

            def link(ins):
                own[0] += 1
                ins.then_inc(act_own, 1)
                act.wait_ge(act_own, own[0])

            def split_hi(u):
                act.wait_ge(raw_loaded[u % RAW_RING], 16 * (u // RAW_RING + 1) + (16 if u % RAW_RING == 0 else 0))
                if u >= SPLIT_RING:
                    wait_unit_used(act, u - SPLIT_RING)
                n = unit_width(u)
                nc.scalar.activation(w_hi[:, u % SPLIT_RING, 0:n], w_raw[:, u % RAW_RING, 0:n], ACT.Copy).then_inc(
                    hi_ready, 1)

            def copy_out(key, dst, func=ACT.Copy, src=None, **kw):
                wait_full(act, key)
                nc.scalar.activation(dst, at_bank(key)[:, :] if src is None else src, func, **kw).then_inc(free(key), 1)

            for t in range(NT):
                act.wait_ge(x_loaded[t], 16)
                if t:
                    act.wait_ge(x_squared, t)
                nc.scalar.activation(junk, x_sb[:, t, :], ACT.Square, accum_out=ss_x[:, t:t + 1]).then_inc(x_squared, 1)
            for s in plan:
                kind, a = s[0], s[1:]
                if kind == "ln_cols":
                    copy_out(s, ln_cols[:, :], src=at_bank(s)[:, 0:KT])
                elif kind == "cols":
                    copy_out(s, cols[:, :], src=at_bank(s)[:, 0:ROWS])
                elif kind == "xT":
                    if a[0] == 0:
                        wait_out(act, ("ln_cols",))
                    wait_full(act, s)
                    nc.scalar.activation(in_hi[:, a[0], :], at_bank(s)[:, :], ACT.Copy,
                                         scale=ln_cols[:, a[0]:a[0] + 1]).then_inc(in_hi_ready, 1)
                    if a[0] in (0, KT - 1):
                        split_hi(a[0] // (KT - 1))
                elif kind == "main":
                    if a[0] + AHEAD < len(UNITS):
                        split_hi(a[0] + AHEAD)
                elif kind == "evac":
                    name = a[0]
                    for j in range(tiles(name)):
                        key = (name, j)
                        if name == "misc":
                            copy_out(key, miscT, src=at_bank(key)[0:MISC, :])
                        elif name == "iq":
                            if j == 0:
                                wait_full(act, ("kiT",))
                            copy_out(key, iqT[:, j, :], src=at_bank(key)[:, 0:SEQ - P])
                        elif name in ("ak", "aq"):
                            copy_out(key, qk_raw[:, j, :])
                        elif name == "av":
                            copy_out(key, v_sb[:, j, :])
                        elif name == "ag":
                            copy_out(key, gate[:, j, 0:GW], ACT.Silu)
                        elif name == "dz":
                            copy_out(key, gate[:, j, GW:D], ACT.Silu)
                        elif name in ("dk", "dq", "dv"):
                            n = ("dk", "dq", "dv").index(name)
                            if n:
                                act.wait_ge(conv_done, 4 * (n - 1) + j + 1)
                            copy_out(key, conv_in[:, j, 3:])
                elif kind == "miscT":
                    copy_out(s, misc[:, :, :].rearrange("p t n -> p (t n)"), src=at_bank(s)[:, 0:NT * MISC])
                elif kind == "gates":
                    act.wait_ge(gate_in, 1)
                    link(nc.scalar.activation(e_nab, nab, ACT.Exp))
                    nc.scalar.activation(ln_sp, e_nab, ACT.Ln, bias=1.0).then_inc(gate_exp, 1)
                    nc.scalar.activation(e_b, misc[:, :, 72:76], ACT.Exp, scale=-1.0).then_inc(gate_exp, 1)
                    act.wait_ge(par_loaded, 16 * 3)
                    nc.scalar.activation(exp_alog, alog_bc, ACT.Exp).then_inc(gate_exp, 1)
                elif kind == "gcum":
                    act.wait_ge(gcum_ready, 1)
                    nc.scalar.activation(e_g, gc, ACT.Exp).then_inc(gcum_exp, 1)
                    nc.scalar.activation(e_last, g_last, ACT.Exp).then_inc(gcum_exp, 1)
                    nc.scalar.activation(e_diff, diff, ACT.Exp).then_inc(gcum_exp, 1)
                elif kind == "idx":
                    n = (a[0] + 1) * P
                    if nth[s] >= 2:
                        act.wait_ge(idx_added, nth[s] - 1)
                    copy_out(s, relu[:, nth[s] % 2, 0:n], ACT.Relu, src=at_bank(s)[:, 0:n])
                elif kind == "norm":
                    for t in range(NT):
                        n = nth[s] * NT + t
                        wait_out(act, (a[0], t))
                        if n >= 2:
                            act.wait_ge(qk_summed, n - 1)
                        nc.scalar.activation(masked[:, n % 2, :], qk_raw[:, t, :], ACT.Square).then_inc(qk_squared, 1)
                elif kind in ("kT", "qT"):
                    c = R_WK if kind == "kT" else R_WQ
                    copy_out(s, (kT if kind == "kT" else qT)[:, a[0], :], scale=cols[:, c:c + 1])
                elif kind == "qk":
                    i = a[0]
                    n = (i // AH + 1) * P
                    act.wait_ge(nmx_ready, i + 1)
                    if i >= 2:
                        wait_full(act, ("pt", i - 2))
                    nc.scalar.activation(prob[:, i % 2, 0:n], masked[:, i % 2, 0:n], ACT.Exp, bias=nmx[:, i:i + 1],
                                         scale=AD ** -0.5, accum_out=p_sum[:, i:i + 1]).then_inc(exp_done, 1)
                elif kind == "pt":
                    i = a[0]
                    n = (i // AH + 1) * P
                    if i % 2 == 0:
                        if i >= 2:
                            wait_av(act, i - 2)
                        copy_out(s, probT[:, i % 2, 0:n], src=at_bank(s)[:, 0:n])
                elif kind == "silu":
                    n = ("dk", "dq", "dv").index(a[0])
                    for j in range(4):
                        act.wait_ge(conv_done, 4 * n + j + 1)
                        y = conv_out[:, 4 * n + j, :]
                        nc.scalar.activation(y, y, ACT.Silu).then_inc(conv_silu, 1)
                elif kind == "dA":
                    c = a[0]
                    for i, x_ in enumerate("kq"):
                        wait_full(act, (x_, c))
                        if c or i:
                            act.wait_ge(d_summed, 2 * c + i)
                        nc.scalar.activation(sq, at_bank((x_, c))[:, :], ACT.Square).then_inc(d_squared, 1)
                elif kind == "dB":
                    c = a[0]
                    if c:
                        wait_full(act, ("kk", c - 1, 1))
                    copy_out(("knT", c), kqT[:, :, 0, :], src=heads(at_bank(("knT", c))[:, :]))
                    copy_out(("qnT", c), kqT[:, :, 1, :], src=heads(at_bank(("qnT", c))[:, :]))
                    copy_out(("qeT", c), qeT[:, c, :, :], src=heads(at_bank(("qeT", c))[:, :]))
                elif kind == "dec":
                    c = a[0]
                    act.wait_ge(gcum_done, 1)
                    act.wait_ge(att_mixed, NT)
                    wait_full(act, s)
                    for h in range(DH):
                        ins = nc.scalar.activation(a_neg[:, c, h, :], at_bank(s)[:, h * P:(h + 1) * P], ACT.Exp,
                                                   bias=gc[:, c * DH + h:c * DH + h + 1], scale=-1.0)
                    ins.then_inc(free(s), 1)
                elif kind == "decT":
                    copy_out(s, intraT[:, a[0], :, :], src=heads(at_bank(s)[:, :]))
                elif kind == "ones":
                    for x_ in "kqv":
                        wait_full(act, (x_, NT - 1))
                    nc.scalar.activation(heads(zc[:, 1, a[0], :]), ident.unsqueeze(1).to_broadcast([P, DH, P]),
                                         ACT.Copy).then_inc(zc_ones_a, 1)
                elif kind == "TU":
                    c, l = a
                    keys = [k for k in (("T", c, l), ("U", c, l)) if k in use]
                    for key in keys:
                        wait_full(act, key)
                    for key in keys:
                        dst = inv_t if key[0] == "T" else inv_u
                        copy_out(key, dst[:, c % 2, :, :], src=heads(at_bank(key)[:, :]))
                elif kind == "uw":
                    copy_out(("w", a[0]), k_bg[:, a[0], :, :], src=heads(at_bank(("w", a[0]))[:, :]))
                elif kind == "onorm":
                    c = a[0]
                    wait_full(act, ("o", c))
                    if c:
                        act.wait_ge(delta_mixed, c)
                    nc.scalar.activation(sq, at_bank(("o", c))[:, :], ACT.Square).then_inc(o_squared, 1)
                elif kind == "mixT":
                    wait_full(act, s)
                    nc.scalar.activation(in_hi[:, a[0], :], at_bank(s)[:, :], ACT.Copy).then_inc(in_hi_ready, 1)

        @block.vector
        def _(dve):
            own = [0]

            def link(ins):
                own[0] += 1
                ins.then_inc(vec, 1)
                dve.wait_ge(vec, own[0])

            def variance(key, src, scale):
                lo, hi = norm_at[key]
                nc.vector.tensor_scalar(var[:, lo:hi], src, scale, EPS, ALU.mult, ALU.add).then_inc(var_ready, 1)

            def root(key):
                lo, hi = norm_at[key]
                dve.wait_ge(rstd_ready, norm_no[key] + 1)
                return rstd[:, lo:hi]

            variance_x = [0]
            for t in range(NT + 1):
                if t < NT:
                    dve.wait_ge(x_squared, t + 1)
                    variance(("x", t), ss_x[:, t:t + 1], 1.0 / D)
                if t:
                    r = root(("x", t - 1))
                    nc.vector.tensor_scalar(x_sb[:, t - 1, :], x_sb[:, t - 1, :], r, None, ALU.mult).then_inc(
                        x_normed, 1)
            for s in plan:
                kind, a = s[0], s[1:]
                if kind in ("xT", "mixT"):
                    k = a[0]
                    dve.wait_ge(in_hi_ready, nth[s] + 1 + (KT if kind == "mixT" else 0))
                    hi = in_hi[:, k, :].bitcast(F32)
                    if kind == "xT":
                        wait_out(dve, ("ln_cols",))
                        ins = nc.vector.scalar_tensor_tensor(in_lo[:, k, :], at_bank(s)[:, :],
                                                             ln_cols[:, k:k + 1], hi, ALU.mult, ALU.subtract)
                    else:
                        ins = nc.vector.tensor_tensor(in_lo[:, k, :], at_bank(s)[:, :], hi, ALU.subtract)
                    ins.then_inc(free(s), 1)
                elif kind == "gates":
                    wait_out(dve, ("miscT",))
                    dve.wait_ge(par_loaded, 16 * 3)
                    link(nc.vector.tensor_tensor(y_dt, misc[:, :, 76:80], dt_bc.unsqueeze(1).to_broadcast([P, NT, DH]),
                                                 ALU.add))
                    nc.vector.scalar_tensor_tensor(nab, y_dt, -1.0, y_dt, ALU.mult, ALU.min).then_inc(gate_in, 1)
                    ik = misc[:, :, 0:AD]
                    link(nc.vector.tensor_reduce(mu_s, ik, AX.X, ALU.add))
                    link(nc.vector.tensor_scalar(mu, mu_s, 1.0 / AD, None, ALU.mult))
                    link(nc.vector.tensor_tensor(ik_c, ik, over(mu, AD), ALU.subtract))
                    link(nc.vector.tensor_tensor(ik_sq, ik_c, ik_c, ALU.mult))
                    link(nc.vector.tensor_reduce(ss_ik, ik_sq, AX.X, ALU.add))
                    variance(("ik",), ss_ik, 1.0 / AD)
                    nc.vector.tensor_scalar(w_i, misc[:, :, 64:72], AH ** -0.5 * AD ** -0.5, None, ALU.mult)
                    dve.wait_ge(gate_exp, 3)
                    link(nc.vector.tensor_scalar(beta, e_b, 1.0, None, ALU.add))
                    link(nc.vector.reciprocal(beta, beta))
                    nc.vector.tensor_scalar(nbeta, beta, -1.0, None, ALU.mult)
                    link(nc.vector.scalar_tensor_tensor(soft, y_dt, 0.0, ln_sp, ALU.max, ALU.add))
                    nc.vector.scalar_tensor_tensor(g, soft, -1.0, exp_alog.unsqueeze(1).to_broadcast([P, NT, DH]),
                                                   ALU.mult, ALU.mult).then_inc(g_ready, 1)
                    r = root(("ik",))
                    for i in range(2):
                        nc.vector.tensor_tensor(ik_n[:, :, i * AD:(i + 1) * AD], ik_c, over(r, AD), ALU.mult).then_inc(
                            ik_ready, 1)
                elif kind == "kiT":
                    wait_out(dve, ("cols",))
                    dve.wait_ge(masks_loaded, 16)
                    nc.vector.tensor_copy(level_mask[:, :, :].rearrange("p l n -> p (l n)"),
                                          mask_words[:, 0:LEVELS * P]).then_inc(masks_cast, 1)
                    nc.vector.tensor_copy(cbf[:, :], mask_words[:, LEVELS * P:]).then_inc(masks_cast, 1)
                    wait_full(dve, s)
                    nc.vector.tensor_scalar(kiT, at_bank(s)[:, :], cols[:, R_IW:R_IW + 1], cols[:, R_IB:R_IB + 1],
                                            ALU.mult, ALU.add).then_inc(free(s), 1)
                elif kind == "gcum":
                    wait_full(dve, s)
                    nc.vector.tensor_copy(gc2, at_bank(s)[:, 0:32]).then_inc(free(s), 1)
                    wait_out(dve, s)
                    nc.vector.tensor_tensor(diff, g_last, gc, ALU.subtract).then_inc(gcum_ready, 1)
                    dve.wait_ge(gcum_exp, 3)
                    nc.vector.tensor_tensor(b_eg, beta.rearrange("p t h -> p (t h)"), e_g, ALU.mult).then_inc(
                        gcum_done, 1)
                elif kind == "idx":
                    qb, h = a
                    n = (qb + 1) * P
                    wait_out(dve, s)
                    r, w = relu[:, nth[s] % 2, 0:n], w_i[:, qb, h:h + 1]
                    if h == 0:
                        ins = nc.vector.tensor_scalar(score[:, qb, 0:n], r, w, None, ALU.mult)
                    else:
                        dve.wait_ge(idx_added, nth[s])
                        ins = nc.vector.scalar_tensor_tensor(score[:, qb, 0:n], r, w, score[:, qb, 0:n], ALU.mult,
                                                             ALU.add)
                    ins.then_inc(idx_added, 1)
                elif kind == "topk":
                    qb, part_ = a
                    sc = score[:, qb, 0:(qb + 1) * P]
                    if part_ == 0:
                        dve.wait_ge(causal_done, qb)
                    for _ in range(TOPK // 8 // 4):
                        link(nc.vector.max(top8, sc))
                        link(nc.vector.match_replace(sc, top8, sc, TAKEN))
                    if part_ == 3:
                        nc.vector.tensor_scalar(sc, sc, 0.97 * TAKEN, NEG, ALU.is_gt, ALU.mult).then_inc(kept_ready, 1)
                elif kind == "norm":
                    for t in range(NT):
                        n = nth[s] * NT + t
                        dve.wait_ge(qk_squared, n + 1)
                        nc.vector.tensor_reduce(ss_att[:, t, :], masked[:, n % 2, :].rearrange(
                            "p (h d) -> p h d", h=AH), AX.X, ALU.add).then_inc(qk_summed, 1)
                    dve.wait_ge(qk_summed, (nth[s] + 1) * NT)
                    variance((a[0],), ss_att.rearrange("p t h -> p (t h)"), 1.0 / AD)
                elif kind == "scale":
                    r = root((a[0],))
                    raw_heads = [qk_raw[:, t, :].rearrange("p (h d) -> p h d", h=AH) for t in range(NT)]
                    for t in range(NT):
                        nc.vector.tensor_tensor(raw_heads[t], raw_heads[t], over(r[:, t * AH:(t + 1) * AH], AD),
                                                ALU.mult).then_inc(qk_normed, 1)
                elif kind == "qk":
                    i = a[0]
                    qb = i // AH
                    n = (qb + 1) * P
                    wait_full(dve, s)
                    if i >= 2:
                        dve.wait_ge(exp_done, i - 1)
                    if i == 0:
                        dve.wait_ge(pool_const, 5)
                    else:
                        dve.wait_ge(kept_ready, qb) if qb else None
                    nc.vector.tensor_tensor_reduce(masked[:, i % 2, 0:n], at_bank(s)[:, 0:n], score[:, qb, 0:n], 1.0,
                                                   TAKEN, ALU.add, ALU.max, mx[:, i:i + 1]).then_inc(free(s), 1)
                    wait_out(dve, s)
                    nc.vector.tensor_scalar(nmx[:, i:i + 1], mx[:, i:i + 1], -AD ** -0.5, None, ALU.mult).then_inc(
                        nmx_ready, 1)
                elif kind == "pt":
                    i = a[0]
                    n = (i // AH + 1) * P
                    if i % 2:
                        if i >= 2:
                            wait_av(dve, i - 2)
                        wait_full(dve, s)
                        nc.vector.tensor_copy(probT[:, i % 2, 0:n], at_bank(s)[:, 0:n]).then_inc(free(s), 1)
                elif kind == "omix":
                    qb = a[0]
                    dve.wait_ge(exp_done, (qb + 1) * AH)
                    link(nc.vector.reciprocal(r_sum, p_sum[:, qb * AH:(qb + 1) * AH]))
                    wait_full(dve, ("O", qb))
                    nc.vector.tensor_tensor(att_out.rearrange("p (h d) -> p h d", h=AH),
                                            bank[7][:, :].rearrange("p (h d) -> p h d", h=AH), over(r_sum, AD),
                                            ALU.mult).then_inc(free(("O", qb)), 1)
                    wait_out(dve, ("O", qb))
                    wait_out(dve, ("ag", qb))
                    nc.vector.tensor_tensor(gate[:, qb, 0:GW], att_out, gate[:, qb, 0:GW], ALU.mult).then_inc(
                        att_mixed, 1)
                elif kind == "conv":
                    name, j = a
                    n = ("dk", "dq", "dv").index(name)
                    wait_out(dve, (name, j))
                    if n == 0 and j == 0:
                        dve.wait_ge(pool_const, 3)
                    y = conv_out[:, 4 * n + j, :]
                    tile = ("dq", "dk", "dv").index(name) * 4 + j

                    def tap(i):
                        c = R_CONV + 12 * i + tile
                        return cols[:, c:c + 1]

                    link(nc.vector.tensor_scalar(y, conv_in[:, j, 0:SEQ], tap(0), None, ALU.mult))
                    for i in range(1, TAPS):
                        ins = nc.vector.scalar_tensor_tensor(y, conv_in[:, j, i:i + SEQ], tap(i), y, ALU.mult, ALU.add)
                        if i < TAPS - 1:
                            link(ins)
                    ins.then_inc(conv_done, 1)
                elif kind == "dA":
                    c = a[0]
                    for i, x_ in enumerate("kq"):
                        dve.wait_ge(d_squared, 2 * c + i + 1)
                        nc.vector.tensor_reduce(ss_d[:, i * DH:(i + 1) * DH], heads(sq), AX.X, ALU.add).then_inc(
                            d_summed, 1)
                    dve.wait_ge(d_summed, 2 * c + 2)
                    variance(("dqk", c), ss_d, 1.0)
                    wait_full(dve, ("v", c))
                    nc.vector.tensor_tensor(v_b[:, c, :, :], heads(at_bank(("v", c))[:, :]), over(beta[:, c, :], DD),
                                            ALU.mult).then_inc(free(("v", c)), 1)
                    r = root(("dqk", c))
                    if c:
                        wait_full(dve, ("qnT", c - 1))
                        dve.wait_ge(d_scaled, 3 * c)
                    nc.vector.tensor_tensor(k_n, heads(at_bank(("k", c))[:, :]), over(r[:, 0:DH], DD),
                                            ALU.mult).then_inc(free(("k", c)), 1)
                    link(nc.vector.tensor_scalar(r_q, r[:, DH:2 * DH], DD ** -0.5, None, ALU.mult))
                    nc.vector.tensor_tensor(q_n, heads(at_bank(("q", c))[:, :]), over(r_q, DD),
                                            ALU.mult).then_inc(free(("q", c)), 1)
                elif kind == "dC":
                    c = a[0]
                    wait_out(dve, ("decT", c))
                    for b in range(2):
                        key = ("kk", c, b)
                        wait_full(dve, key)
                        src = at_bank(key)[:, :].rearrange("p (h x n) -> p h x n", h=2, x=2)
                        for i in range(2):
                            h = 2 * b + i
                            ins = nc.vector.scalar_tensor_tensor(a_neg[:, c, h, :], src[:, i, 0, :], nbeta[:, c, h:h + 1],
                                                           a_neg[:, c, h, :], ALU.mult, ALU.mult)
                        ins.then_inc(kk_done, 1)
                        nc.vector.tensor_tensor(intraT[:, c, 2 * b:2 * b + 2, :], src[:, :, 1, :],
                                                intraT[:, c, 2 * b:2 * b + 2, :], ALU.mult).then_inc(free(key), 1)
                elif kind == "ones":
                    for x_ in "kqv":
                        wait_full(dve, (x_, NT - 1))
                    nc.vector.tensor_copy(heads(zc[:, 0, a[0], :]),
                                          ident.unsqueeze(1).to_broadcast([P, DH, P])).then_inc(zc_ones_v, 1)
                elif kind == "Z":
                    c, l = a
                    wait_full(dve, s)
                    dve.wait_ge(zc_ones_a if c % 2 else zc_ones_v, l + 1)
                    dve.wait_ge(masks_cast, 1)
                    nc.vector.copy_predicated(heads(zc[:, c % 2, l, :]),
                                              level_mask[:, l, :].unsqueeze(1).to_broadcast([P, DH, P]),
                                              heads(at_bank(s)[:, :])).then_inc(free(s), 1)
                elif kind == "TU" and a[1] < LEVELS - 2:
                    c, l = a
                    if l:
                        wait_out(dve, ("U", c, l))
                    else:
                        wait_out(dve, ("Z", c, 0))
                        if c > 1:
                            wait_full(dve, ("U", c - 2, LEVELS - 1))
                    src = inv_u[:, c % 2, :, :].rearrange("p h n -> p (h n)") if l else zc[:, c % 2, 0, :]
                    nc.vector.transpose(inv_t[:, c % 2, :, :].rearrange("p h n -> p (h n)"), src).then_inc(t_ready, 1)
                elif kind == "uw":
                    wait_full(dve, ("u", a[0]))
                    nc.vector.tensor_copy(v_b[:, a[0], :, :], heads(at_bank(("u", a[0]))[:, :])).then_inc(
                        free(("u", a[0])), 1)
                elif kind == "ws" and a[0] > 0:
                    c = a[0]
                    wait_full(dve, s)
                    wait_out(dve, ("u", c))
                    nc.vector.tensor_tensor(v_new[:, c % 2, :, :], v_b[:, c, :, :], heads(at_bank(s)[:, :]),
                                            ALU.subtract).then_inc(free(s), 1)
                elif kind == "kv" and a[0] < NT - 1:
                    c = a[0]
                    wait_full(dve, s)
                    if c == 0:
                        nc.vector.tensor_copy(state[:, 1, :, :], heads(at_bank(s)[:, :])).then_inc(free(s), 1)
                    else:
                        wait_out(dve, ("kv", c - 1))
                        for h in range(DH):
                            ins = nc.vector.scalar_tensor_tensor(
                                state[:, (c + 1) % 2, h, :], state[:, c % 2, h, :],
                                e_last[:, c * DH + h:c * DH + h + 1], at_bank(s)[:, h * P:(h + 1) * P], ALU.mult, ALU.add)
                        ins.then_inc(free(s), 1)
                elif kind == "onorm":
                    c = a[0]
                    dve.wait_ge(o_squared, c + 1)
                    link(nc.vector.tensor_reduce(ss_d[:, 0:DH], heads(sq), AX.X, ALU.add))
                    variance(s, ss_d[:, 0:DH], 1.0 / DD)
                    r = root(s)
                    nc.vector.tensor_tensor(heads(o_tmp), heads(at_bank(("o", c))[:, :]), over(r, DD),
                                            ALU.mult).then_inc(free(("o", c)), 1)
                    wait_out(dve, ("o", c))
                    dve.wait_ge(dz_scaled, c + 1)
                    nc.vector.tensor_tensor(gate[:, c, GW:D], o_tmp, gate[:, c, GW:D], ALU.mult).then_inc(
                        delta_mixed, 1)
                elif kind == "evac" and a[0][:3] == "out":
                    n = int(a[0][3])
                    if n == 0:
                        dve.wait_ge(x_again, 16 * NT)
                    for j in range(4):
                        key = (a[0], j)
                        wait_full(dve, key)
                        y = x_sb[:, j, n * GW:(n + 1) * GW]
                        nc.vector.tensor_tensor(y, at_bank(key)[:, :], y, ALU.add).then_inc(free(key), 1)

        @block.gpsimd
        def _(pool):
            def split_lo(u):
                pool.wait_ge(hi_ready, u + 1)
                if u >= SPLIT_RING:
                    wait_unit_used(pool, u - SPLIT_RING)
                n = unit_width(u)
                nc.gpsimd.tensor_tensor(w_lo[:, u % SPLIT_RING, 0:n], w_raw[:, u % RAW_RING, 0:n],
                                        w_hi[:, u % SPLIT_RING, 0:n].bitcast(F32), ALU.subtract).then_inc(lo_ready, 1)

            def power(key):
                lo, hi = norm_at[key]
                pool.wait_ge(var_ready, norm_no[key] + 1)
                nc.gpsimd.tensor_tensor(rstd[:, lo:hi], var[:, lo:hi], half[:, 0:hi - lo], ALU.pow).then_inc(
                    rstd_ready, 1)

            nc.gpsimd.memset(half[:, :], -0.5).then_inc(pool_const, 1)
            pool.dma_start(rows[R_CONV:R_CONV + 48, :], conv_w.rearrange("a j (n p) -> (a j n) p", p=P)).then_inc(
                rows_loaded, 16)
            for r, w in ((R_WQ, wq_n), (R_WK, wk_n), (R_IW, wi_n), (R_IB, bi_n)):
                pool.dma_start(rows[r:r + 1, :].rearrange("a (b d) -> a b d", b=2),
                              w.unsqueeze(1).to_broadcast([1, 2, AD])).then_inc(rows_loaded, 16)
            pool.dma_start(alog_bc, a_log.to_broadcast([P, DH])).then_inc(par_loaded, 16)
            pool.dma_start(dt_bc, dt_b.to_broadcast([P, DH])).then_inc(par_loaded, 16)
            pool.dma_start(dnw[:, :], dn_w.to_broadcast([P, DD])).then_inc(par_loaded, 16)
            nc.gpsimd.memset(ones[:, :], 1.0).then_inc(pool_const, 1)
            nc.gpsimd.memset(conv_in[:, :, 0:TAPS - 1], 0.0).then_inc(pool_const, 1)
            first = score[:, 0, 0:P]
            nc.gpsimd.memset(first, 0.0).then_inc(pool_const, 1)
            pool.wait_ge(pool_const, 4)
            nc.gpsimd.affine_select(out=first, in_=first, compare_op=ALU.is_ge, fill=NEG, base=0, pattern=[[-1, P]],
                                    channel_multiplier=1).then_inc(pool_const, 1)
            for t in range(NT):
                power(("x", t))
            split_lo(0)
            split_lo(1)
            for s in plan:
                kind, a = s[0], s[1:]
                if kind == "main":
                    if a[0] + AHEAD < len(UNITS):
                        split_lo(a[0] + AHEAD)
                elif kind == "gates":
                    power(("ik",))
                elif kind == "causal":
                    qb = a[0]
                    d = score[:, qb, qb * P:(qb + 1) * P]
                    pool.wait_ge(idx_added, qb * AH)
                    nc.gpsimd.affine_select(out=d, in_=d, compare_op=ALU.is_ge, fill=NEG, base=0, pattern=[[-1, P]],
                                            channel_multiplier=1).then_inc(causal_done, 1)
                elif kind == "norm":
                    power((a[0],))
                elif kind == "dA":
                    c = a[0]
                    power(("dqk", c))
                    sl = slice(c * DH, (c + 1) * DH)
                    wait_out(pool, ("q", c))
                    if c == 0:
                        pool.wait_ge(gcum_done, 1)
                    else:
                        wait_full(pool, ("qeT", c - 1))
                    nc.gpsimd.tensor_tensor(q_e, q_n, over(e_g[:, sl], DD), ALU.mult).then_inc(d_scaled, 1)
                    wait_out(pool, ("k", c))
                    nc.gpsimd.tensor_tensor(k_bg[:, c, :, :], k_n, over(b_eg[:, sl], DD), ALU.mult).then_inc(d_scaled, 1)
                    nc.gpsimd.tensor_tensor(k_dec[:, c, :, :], k_n, over(e_diff[:, sl], DD), ALU.mult).then_inc(
                        d_scaled, 1)
                elif kind == "evac" and a[0] == "dz":
                    for j in range(4):
                        wait_out(pool, ("dz", j))
                        y = heads(gate[:, j, GW:D])
                        nc.gpsimd.tensor_tensor(y, y, dnw[:, :].unsqueeze(1).to_broadcast([P, DH, DD]),
                                                ALU.mult).then_inc(dz_scaled, 1)
                elif kind == "onorm":
                    power(s)


def constants():
    i = np.arange(P)
    row, col = i[:, None], i[None, :]
    levels = [((row >> (l + 1)) == (col >> (l + 1))) & ((row >> l) % 2 == 0) & ((col >> l) % 2 == 1)
              for l in range(LEVELS)]
    lower = np.where(col <= row, 0.0, -NEG)
    return np.concatenate([row == col, row <= col, *levels, row == col, lower], axis=1).astype(np.float32)


_INS = ["x", "ln_w", "w_in", "attn_q_norm_w", "attn_k_norm_w", "idx_k_norm_w", "idx_k_norm_b", "dn_conv_w", "dn_A_log",
        "dn_dt_bias", "dn_norm_w", "w_out"]


def kernel(**inputs):
    import concourse.bacc as bacc
    from concourse.bass_utils import run_bass_kernel_spmd

    nc = bacc.Bacc("TRN2", target_bir_lowering=False, num_devices=1)
    arrays = {f"in_{n}": np.ascontiguousarray(inputs[n]) for n in _INS}
    arrays["constants"] = constants()
    args = [nc.dram_tensor(n, a.shape, mybir.dt.from_np(a.dtype), kind="ExternalInput").ap()
            for n, a in arrays.items()]
    out = nc.dram_tensor("out", (1, SEQ, D), F32, kind="ExternalOutput").ap()
    build(nc, *args, out)
    result = run_bass_kernel_spmd(nc, [arrays], core_ids=[0])
    return result.results[0]["out"]
```

```python
from contextlib import ExitStack

import numpy as np

import concourse.bass as bass
from concourse import mybir

F32 = mybir.dt.float32
F32R = mybir.dt.float32r
BF16 = mybir.dt.bfloat16
U8 = mybir.dt.uint8
ALU = mybir.AluOpType
ACT = mybir.ActivationFunctionType
AX = mybir.AxisListType

P = 128
SEQ = 512
D = 1024
NT = SEQ // P
KT = D // P
AH, AD = 8, 64
DH, DD = 4, 128
TOPK = min(256, SEQ // 4)
TAPS = 4
EPS = 1e-6
NEG = -1e30
TAKEN = -3e38
LEVELS = 7
MASKED = 5
GW = 512

C_AQ, C_AK, C_AV, C_AG, C_IQ, C_IK = 0, 512, 1024, 1536, 2048, 2560
C_DQ, C_DK, C_DV, C_DZ, C_DB = 2632, 3144, 3656, 4168, 4680
MISC = 80

GROUPS = [
    ("misc", "B", C_IK, SEQ), ("iq", "B", C_IQ, SEQ - P), ("ak", "A", C_AK, GW), ("aq", "A", C_AQ, GW),
    ("av", "A", C_AV, GW), ("ag", "B", C_AG, SEQ), ("dk", "B", C_DK, SEQ), ("dq", "B", C_DQ, SEQ),
    ("dv", "B", C_DV, SEQ), ("dz", "A", C_DZ, GW), ("out0", "A", 0, GW), ("out1", "A", GW, GW),
]
GROUP = {g[0]: g for g in GROUPS}
UNITS = [("misc", tuple(range(KT)))] + [(g[0], (k, k + 1)) for g in GROUPS[1:] for k in range(0, KT, 2)]
RAW_RING, SPLIT_RING, AHEAD = 4, 3, 2

R_CONV, R_WQ, R_WK, R_IW, R_IB, ROWS = 0, 48, 49, 50, 51, 52


def tiles(name):
    return 1 if name == "misc" else 4


def make_plan():
    plan = [("ln_cols",)] + [("x", t) for t in range(NT)] + [("xT", k) for k in range(KT)]

    def unit(name, n):
        plan.append(("main", UNITS.index((name, tuple(range(KT)) if name == "misc" else (2 * n, 2 * n + 1)))))
        if n == 3 or name == "misc":
            plan.append(("evac", name))

    unit("misc", 0)
    plan.append(("cols",))
    unit("iq", 0)
    plan.extend([("miscT",), ("gates",)])
    for n in range(1, 4):
        unit("iq", n)
    plan.extend([("kiT",), ("gcum",)])
    idx = [("idx", qb, h) for qb in range(1, NT) for h in range(AH)]
    for n in range(4):
        unit("ak", n)
        for s in idx[6 * n:6 * n + 6]:
            plan.append(s)
            if s[2] == AH - 1:
                plan.append(("causal", s[1]))
    plan.append(("norm", "ak"))
    for n in range(4):
        unit("aq", n)
        plan.append(("topk", 1, n, 4))
        if n == 0:
            plan.append(("root", "ak"))
        if n == 1:
            plan.append(("scale", "ak"))
        if n == 2:
            plan.extend([("kT", j) for j in range(4)])
    plan.append(("norm", "aq"))
    for n in range(4):
        unit("av", n)
        plan.append(("topk", 2, n, 4))
        if n == 0:
            plan.append(("root", "aq"))
        if n == 1:
            plan.append(("scale", "aq"))
        if n == 2:
            plan.extend([("qT", j) for j in range(4)])
    att = []
    n_att = NT * AH
    for n in range(n_att + 4):
        att.append([])
        if 3 <= n < n_att + 3:
            att[-1].append(("pt", n - 3))
        if n < n_att:
            att[-1].append(("qk", n))
        if n >= 4:
            att[-1].append(("av", n - 4))
            if (n - 4) % AH == AH - 1:
                att[-1].append(("omix", (n - 4) // AH))
    at = 0

    def attend(n):
        nonlocal at
        for i, here in enumerate(att[at:at + n]):
            plan.extend(here)
            if i and at + i - 1 < n_att:
                plan.append(("pn", at + i - 1))
        at = min(at + n, len(att))
        if at - 1 < n_att:
            plan.append(("pn", at - 1))

    for n in range(4):
        unit("ag", n)
        attend((1, 1, 2, 2)[n])
        plan.append(("topk", 3, n, 8))
    for g, before in (("dk", None), ("dq", "dk"), ("dv", "dq")):
        for n in range(4):
            unit(g, n)
            if before:
                plan.append(("conv", before, n))
            attend(2 if n == 0 else 3)
            if g == "dk":
                plan.append(("topk", 3, 4 + n, 8))
        if before:
            plan.append(("silu", before))
    attend(len(att))
    plan.extend([("conv", "dv", 0), ("conv", "dv", 1)])
    unit("dz", 0)
    plan.extend([("dA", 0), ("dec", 0), ("dec", 1), ("conv", "dv", 2)])
    unit("dz", 1)
    plan.extend([("dS", 0), ("dB", 0), ("conv", "dv", 3), ("decT", 0), ("dec", 2), ("dec", 3), ("dA", 1), ("dS", 1), ("silu", "dv")])
    unit("dz", 2)
    plan.extend([("dE", 0), ("dC", 0), ("dB", 1), ("decT", 1), ("decT", 2), ("dA", 2), ("dA", 3), ("dS", 2), ("dS", 3)])
    unit("dz", 3)
    plan.extend([("dE", 1), ("dC", 1), ("dB", 2), ("allbanks",), ("dV", 0), ("dV", 1), ("dV", 2), ("dV", 3),
                 ("ones", 0)])
    mix = {0: ("decT", 3), 1: ("dC", 2), 2: ("dE", 2), 3: ("dB", 3), 4: ("dC", 3), 5: ("dE", 3)}
    for l in range(LEVELS):
        plan.extend([("Z", c, l) for c in (0, 1)])
        if l + 1 < MASKED:
            plan.append(("ones", l + 1))
        if l in mix:
            plan.append(mix[l])
        plan.extend([("TU", c, l) for c in (0, 1)])
    plan.extend([("uw", c) for c in (0, 1)])
    plan.extend([("dzw", t) for t in range(NT)] + [("mixC", k) for k in range(KT // 2)])
    mix = {0: ("kv", 0), 1: ("o", 0), 2: ("oscale", 0), 3: ("ws", 1), 5: ("kv", 1), 6: ("o", 1)}
    for l in range(LEVELS):
        plan.extend([("Z", c, l) for c in (2, 3)])
        if l in mix:
            plan.append(mix[l])
        plan.extend([("TU", c, l) for c in (2, 3)])
        if l == 1:
            plan.append(("onorm", 0))
    plan.extend([("onorm", 1), ("uw", 2), ("uw", 3), ("reload",), ("oscale", 1), ("ws", 2), ("kv", 2), ("o", 2), ("ws", 3),
                 ("onorm", 2)])
    unit("out0", 0)
    plan.extend([("o", 3), ("oscale", 2), ("onorm", 3), ("oscale", 3)])
    unit("out0", 1)
    plan.extend([("mixT", k) for k in range(4, 8)])
    for n in (2, 3):
        unit("out0", n)
    for n in range(4):
        unit("out1", n)
    return plan


def assign_banks(plan):
    use, count = {}, [0] * 8
    ring, turn = [4, 5, 6, 7], 0

    def take(key, bank=None):
        nonlocal turn
        if bank is None:
            bank = ring[turn % len(ring)]
            turn += 1
        use[key] = (bank, count[bank])
        count[bank] += 1

    for s in plan:
        kind = s[0]
        if kind == "main":
            name, ks = UNITS[s[1]]
            if ks[0] == 0:
                for j in range(tiles(name)):
                    take((name, j), j)
                if name == "out0":
                    ring = [4, 5, 6, 7]
        elif kind == "allbanks":
            ring = list(range(8))
        elif kind == "qk":
            if s[1] == 0:
                ring = [4, 5, 6]
            take(s)
        elif kind == "ln_cols":
            take(s, 7)
        elif kind == "x":
            if s[1] == 0:
                for k in range(KT):
                    take(("xT", k), k)
        elif kind == "o" and s[1] == 2:
            while ring[turn % len(ring)] < 4:
                turn += 1
            take(s)
        elif kind in ("cols", "miscT", "kiT", "gcum", "idx", "kT", "qT", "pt", "mixT", "o", "Z", "decT"):
            take(s)
        elif kind == "av":
            if s[1] % AH == 0:
                take(("O", s[1] // AH), 7)
        elif kind == "dec":
            take(s)
        elif kind == "dA":
            if s[1] == 0:
                ring = [4, 5, 6, 7]
            for x in "kq":
                take((x, s[1]))
        elif kind == "dV":
            take(("v", s[1]))
        elif kind == "dB":
            for x in ("knT", "qnT"):
                take((x, s[1]))
        elif kind == "dE":
            take(("qeT", s[1]))
        elif kind == "dC":
            for b in range(2):
                take(("kk", s[1], b))
        elif kind == "TU":
            _, c, l = s
            if l == LEVELS - 2:
                take(("T", c, l))
            if l > 0:
                take(("U", c, l))
        elif kind == "uw":
            take(("u", s[1]))
            take(("w", s[1]))
        elif kind == "ws" and s[1] > 0:
            take(s)
        elif kind == "kv" and s[1] < NT - 1:
            take(s)
    return use


def build(nc, x, ln_w, w_in, wq_n, wk_n, wi_n, bi_n, conv_w, a_log, dt_b, dn_w, w_out, c_f32, out):
    plan = make_plan()
    use = assign_banks(plan)
    kinds = {}
    nth = {}
    for s in plan:
        nth[s] = kinds.get(s[0], 0)
        kinds[s[0]] = nth[s] + 1
    norm_at, norm_no, at = {}, {}, 0
    for key, w in ([(("x", t), 1) for t in range(NT)] + [(("ik",), NT), (("ak",), NT * AH), (("aq",), NT * AH)]
                   + [(("dqk", c), 2 * DH) for c in range(NT)] + [(("onorm", c), DH) for c in range(NT)]):
        norm_at[key], norm_no[key] = (at, at + w), len(norm_no)
        at += w
    norm_cols = at

    with ExitStack() as ctx:
        def sb(name, shape, dt=F32):
            return ctx.enter_context(nc.sbuf_tensor(name, shape, dt))

        def sem(name):
            return ctx.enter_context(nc.semaphore(name))

        bank = [ctx.enter_context(nc.psum_tensor(f"bank{i}", [P, 512], F32)) for i in range(8)]

        w_raw = sb("w_raw", [P, RAW_RING, 2 * GW])
        w_hi = sb("w_hi", [P, SPLIT_RING, 2 * GW], F32R)
        w_lo = sb("w_lo", [P, SPLIT_RING, 2 * GW], F32R)
        in_hi = sb("in_hi", [P, KT, SEQ], F32R)
        in_lo = sb("in_lo", [P, KT, SEQ], F32R)
        gate = sb("gate", [P, NT, D])
        arena1 = sb("arena1", [P, 14 * 512])
        arena2 = sb("arena2", [P, 20480])
        consts = sb("consts", [P, 2 * P])
        ident, tri = consts[:, 0:P], consts[:, P:2 * P]
        level_mask = sb("level_mask", [P, MASKED, P], U8)
        cbf = sb("cbf", [P, 2 * P], BF16)
        ident_bf, keep_lower = cbf[:, 0:P], cbf[:, P:2 * P]
        ones = sb("ones", [P, P])
        rows = sb("rows", [ROWS, P])
        ln_rows = sb("ln_rows", [KT, P])
        ln_cols = sb("ln_cols", [P, KT])
        cols = sb("cols", [P, ROWS])
        dnw = sb("dnw", [P, DD])
        small = sb("small", [P, 640])
        var = sb("var", [P, norm_cols])
        rstd = sb("rstd", [P, norm_cols])
        half = sb("half", [P, 32])
        misc = sb("misc", [P, NT, MISC])

        x_sb = arena1[:, 0:4096].rearrange("p (t d) -> p t d", t=NT)
        conv_out = arena1[:, 0:6144].rearrange("p (n t) -> p n t", n=12)
        zc = arena1[:, :].rearrange("p (b l n) -> p b l n", b=2, l=LEVELS)

        mask_words = gate[:, 0:2, :].rearrange("p t d -> p (t d)")[:, 0:(MASKED + 2) * P]

        spot = [0]

        def part(words):
            spot[0] += words
            return arena2[:, spot[0] - words:spot[0]]

        iqT = part(4 * 384).rearrange("p (n t) -> p n t", n=4)
        kiT = part(512)
        qk_raw = part(2048).rearrange("p (t n) -> p t n", t=NT)
        qT = part(2048).rearrange("p (j t) -> p j t", j=4)
        kT = part(2048).rearrange("p (j t) -> p j t", j=4)
        v_sb = part(2048).rearrange("p (t n) -> p t n", t=NT)
        score = part(4 * 512).rearrange("p (q s) -> p q s", q=NT)
        masked = part(2 * 512).rearrange("p (b s) -> p b s", b=2)
        prob = part(3 * 512).rearrange("p (b s) -> p b s", b=3)
        relu = prob
        probT = part(2 * 512).rearrange("p (b s) -> p b s", b=2)
        attention_words = spot[0]
        miscT = prob[0:MISC, 0:2, :].rearrange("p b s -> p (b s)")[:, 0:SEQ]
        conv_in = arena2[:, attention_words:attention_words + 4 * (SEQ + 3)].rearrange("p (j t) -> p j t", j=4)
        junk = arena2[:, 2048:2048 + D]

        spot[0] = 0
        k_dec, k_bg, v_b, qeT, a_neg, intraT = (
            part(2048).rearrange("p (c h n) -> p c h n", c=NT, h=DH) for _ in range(6))
        q_n, k_n = (part(1024).rearrange("p (b h n) -> p b h n", b=2, h=DH) for _ in range(2))
        q_e = part(512).rearrange("p (h n) -> p h n", h=DH)
        kqT = part(1024).rearrange("p (h x n) -> p h x n", h=DH, x=2)
        spot[0] = max(spot[0], attention_words)
        inv_u, inv_t = (part(1024).rearrange("p (b h n) -> p b h n", b=2, h=DH) for _ in range(2))
        state, v_new = (part(1024).rearrange("p (b h n) -> p b h n", b=2, h=DH) for _ in range(2))
        o_tmp = part(512)
        sq = o_tmp
        o_sq = kqT[:, 0, 0, :]
        assert spot[0] <= 20480 and attention_words + 4 * (SEQ + 3) <= spot[0] - 512

        sm = [0]

        def tiny(n):
            sm[0] += n
            assert sm[0] <= 640
            return small[:, sm[0] - n:sm[0]]

        ss_x = tiny(NT)
        w_i = tiny(NT * AH).rearrange("p (t h) -> p t h", t=NT)
        mu, mu_s, ss_ik = tiny(NT), tiny(NT), tiny(NT)
        ss_att = tiny(NT * AH).rearrange("p (t h) -> p t h", t=NT)
        dt_bc, alog_bc, exp_alog = tiny(DH), tiny(DH), tiny(DH)
        y_dt, nab, e_nab, ln_sp, soft, e_b, beta, nbeta, g = (
            tiny(NT * DH).rearrange("p (t h) -> p t h", t=NT) for _ in range(9))
        gc2 = tiny(2 * NT * DH)
        gc, g_last = gc2[:, 0:NT * DH], gc2[:, NT * DH:]
        e_g, e_last, diff, e_diff, b_eg = (tiny(NT * DH) for _ in range(5))
        top8 = tiny(8)
        mx, nmx, p_sum = tiny(NT * AH), tiny(NT * AH), tiny(NT * AH)
        ss_d, r_q, ss_o = tiny(2 * DH), tiny(DH), tiny(DH)
        ik_c = arena2[:, 0:NT * AD].rearrange("p (t d) -> p t d", t=NT)
        ik_sq = arena2[:, 256:256 + NT * AD].rearrange("p (t d) -> p t d", t=NT)
        ik_n = arena2[:, 2048:2048 + NT * P].rearrange("p (t d) -> p t d", t=NT)

        bank_full = [sem(f"bank_full{i}") for i in range(8)]
        bank_free = [sem(f"bank_free{i}") for i in range(8)]
        raw_loaded = [sem(f"raw_loaded{i}") for i in range(RAW_RING)]
        x_loaded = [sem(f"x_loaded{t}") for t in range(NT)]
        const_loaded = sem("const_loaded")
        ln_loaded = sem("ln_loaded")
        masks_cast = sem("masks_cast")
        rows_loaded, par_loaded, masks_loaded = sem("rows_loaded"), sem("par_loaded"), sem("masks_loaded")
        x_again = sem("x_again")
        stored = sem("stored")
        hi_ready, lo_ready, w_used = sem("hi_ready"), sem("lo_ready"), sem("w_used")
        in_hi_ready = sem("in_hi_ready")
        pool_const = sem("pool_const")
        x_squared, x_normed = sem("x_squared"), sem("x_normed")
        var_ready, rstd_ready = sem("var_ready"), sem("rstd_ready")
        vec = sem("vec")
        act_own = sem("act_own")
        ik_ready, gate_in, gate_exp, g_ready = sem("ik_ready"), sem("gate_in"), sem("gate_exp"), sem("g_ready")
        gcum_ready, gcum_exp, gcum_done = sem("gcum_ready"), sem("gcum_exp"), sem("gcum_done")
        idx_added, causal_done, kept_ready = sem("idx_added"), sem("causal_done"), sem("kept_ready")
        qk_squared, qk_summed, qk_normed = sem("qk_squared"), sem("qk_summed"), sem("qk_normed")
        nmx_ready, exp_done, r_ready, prob_normed, av_done = (
            sem(n) for n in ("nmx_ready", "exp_done", "r_ready", "prob_normed", "av_done"))
        mix_hi_ready, mix_lo_ready = sem("mix_hi_ready"), sem("mix_lo_ready")
        conv_done, conv_silu = sem("conv_done"), sem("conv_silu")
        d_squared, d_summed, d_scaled = sem("d_squared"), sem("d_summed"), sem("d_scaled")
        dz_scaled, dec_ready, kk_done = sem("dz_scaled"), sem("dec_ready"), sem("kk_done")
        t_ready = sem("t_ready")
        zc_ones_v, zc_ones_a = sem("zc_ones_v"), sem("zc_ones_a")
        o_squared, o_summed, delta_mixed = sem("o_squared"), sem("o_summed"), sem("delta_mixed")

        def wait_full(eng, key):
            b, before = use[key]
            eng.wait_ge(bank_full[b], before + 1)

        def wait_out(eng, key):
            b, before = use[key]
            eng.wait_ge(bank_free[b], before + 1)

        def wait_bank(eng, key):
            b, before = use[key]
            if before:
                eng.wait_ge(bank_free[b], before)

        def full(key):
            return bank_full[use[key][0]]

        def free(key):
            return bank_free[use[key][0]]

        def at_bank(key):
            return bank[use[key][0]]

        def heads(ap):
            return ap.rearrange("p (h n) -> p h n", h=DH)

        def over(ap, n):
            return ap.unsqueeze(2).to_broadcast([P, ap.shape[1], n])

        def last_unit(u):
            return u == len(UNITS) - 1 or UNITS[u + 1][0] != UNITS[u][0]

        def wait_unit_used(eng, u):
            if last_unit(u):
                wait_full(eng, (UNITS[u][0], tiles(UNITS[u][0]) - 1))
            else:
                eng.wait_ge(w_used, sum(not last_unit(i) for i in range(u + 1)))

        def unit_width(u):
            return KT * MISC if UNITS[u][0] == "misc" else 2 * GW

        def wait_av(eng, i):
            if i % AH == AH - 1:
                wait_full(eng, ("O", i // AH))
            else:
                eng.wait_ge(av_done, i + 1 - (i + 1) // AH)

        def wait_t(eng, c, l):
            if l < LEVELS - 2:
                eng.wait_ge(t_ready, (c // 2 * (LEVELS - 2) + l) * 2 + c % 2 + 1)
            else:
                wait_out(eng, ("T", c, l))

        def blocks(l):
            n = 1 << l
            return [(slice(b, b + n), slice(b + n, b + 2 * n)) for b in range(0, P, 2 * n)]

        block = ctx.enter_context(nc.Block())

        @block.sync
        def _(sp):
            xs = x.rearrange("b (t p) d -> p (b t) d", p=P)
            for t in range(NT):
                sp.dma_start(x_sb[:, t, :], xs[:, t, :]).then_inc(x_loaded[t], 16)
                if t == 1:
                    sp.dma_start(ln_rows[:, :], ln_w.rearrange("a (k p) -> (a k) p", p=P)).then_inc(ln_loaded, 16)
                    sp.dma_start(consts[:, :], c_f32[:, 0:2 * P]).then_inc(const_loaded, 16)
            for u, (name, ks) in enumerate(UNITS):
                r = u % RAW_RING
                if u >= RAW_RING:
                    sp.wait_ge(hi_ready, u - RAW_RING + 1)
                    sp.wait_ge(lo_ready, u - RAW_RING + 1)
                if name == "misc":
                    dst = w_raw[:, r, 0:KT * MISC].rearrange("p (k n) -> p k n", k=KT)
                    src = w_in.rearrange("a (k p) n -> p (a k) n", p=P)
                    sp.dma_start(dst[:, :, 0:72], src[:, :, C_IK:C_IK + 72]).then_inc(raw_loaded[r], 16)
                    sp.dma_start(dst[:, :, 72:80], src[:, :, C_DB:C_DB + 8]).then_inc(raw_loaded[r], 16)
                else:
                    c0 = GROUP[name][2]
                    w = w_out if name[:3] == "out" else w_in
                    src = w.rearrange("a (k p) n -> p (a k) n", p=P)[:, ks[0]:ks[1] + 1, c0:c0 + GW]
                    sp.dma_start(w_raw[:, r, :].rearrange("p (k n) -> p k n", k=2), src).then_inc(raw_loaded[r], 16)
                if u == RAW_RING - 2:
                    sp.dma_start(rows[R_CONV:R_CONV + 48, :], conv_w.rearrange("a j (n p) -> (a j n) p", p=P)).then_inc(
                        rows_loaded, 16)
                    for r, w in ((R_WQ, wq_n), (R_WK, wk_n), (R_IW, wi_n), (R_IB, bi_n)):
                        sp.dma_start(rows[r:r + 1, :].rearrange("a (b d) -> a b d", b=2),
                                      w.unsqueeze(1).to_broadcast([1, 2, AD])).then_inc(rows_loaded, 16)
                    sp.dma_start(alog_bc, a_log.to_broadcast([P, DH])).then_inc(par_loaded, 16)
                    sp.dma_start(dt_bc, dt_b.to_broadcast([P, DH])).then_inc(par_loaded, 16)
                    sp.dma_start(dnw[:, :], dn_w.to_broadcast([P, DD])).then_inc(par_loaded, 16)
                if u == RAW_RING - 1:
                    sp.dma_start(mask_words, c_f32[:, 2 * P:]).then_inc(masks_loaded, 16)
            wait_full(sp, ("U", NT - 1, LEVELS - 1))
            for t in range(NT):
                sp.dma_start(x_sb[:, t, :], xs[:, t, :]).then_inc(x_again, 16)
            os_ = out.rearrange("b (t p) d -> p (b t) d", p=P)
            for n in range(2):
                for t in range(NT):
                    wait_out(sp, (f"out{n}", t))
                    sp.dma_start(os_[:, t, n * GW:(n + 1) * GW], x_sb[:, t, n * GW:(n + 1) * GW]).then_inc(stored, 16)
            sp.wait_ge(stored, 16 * 2 * NT)

        @block.tensor
        def _(pe):
            def transposes(key, srcs):
                wait_bank(pe, key)
                for i, s in enumerate(srcs):
                    ins = nc.tensor.transpose(at_bank(key)[:, i * P:(i + 1) * P], s, ident)
                ins.then_inc(full(key), 1)

            def main(u):
                name, ks = UNITS[u]
                _, layout, _, width = GROUP[name]
                slot = u % SPLIT_RING
                n = MISC if name == "misc" else GW
                hi = w_hi[:, slot, 0:len(ks) * n].rearrange("p (k n) -> p k n", k=len(ks))
                lo = w_lo[:, slot, 0:len(ks) * n].rearrange("p (k n) -> p k n", k=len(ks))
                pe.wait_ge(hi_ready, u + 1)
                pe.wait_ge(lo_ready, u + 1)
                for i, k in enumerate(ks):
                    if name == "misc":
                        wait_out(pe, ("xT", k))
                    if name == "out0":
                        if k < KT // 2:
                            pe.wait_ge(mix_lo_ready, k + 1)
                        else:
                            wait_out(pe, ("mixT", k))
                    for j in range(tiles(name)):
                        if k == 0:
                            wait_bank(pe, (name, j))
                        dst = at_bank((name, j))[0:min(n, P), 0:width]
                        if layout == "A":
                            xh, xl = in_hi[:, k, j * P:(j + 1) * P], in_lo[:, k, j * P:(j + 1) * P]
                            pairs = ((xh, hi[:, i, :]), (xh, lo[:, i, :]), (xl, hi[:, i, :]))
                        else:
                            wh, wl = (x_[:, i, j * P:j * P + min(n, P)] for x_ in (hi, lo))
                            xh, xl = in_hi[:, k, SEQ - width:], in_lo[:, k, SEQ - width:]
                            pairs = ((wh, xh), (wh, xl), (wl, xh))
                        for m, (a, b) in enumerate(pairs):
                            ins = nc.tensor.matmul(dst, a, b, start=(k == 0 and m == 0), stop=(k == KT - 1 and m == 2))
                        if k == KT - 1:
                            ins.then_inc(full((name, j)), 1)
                if not last_unit(u):
                    ins.then_inc(w_used, 1)

            pe.wait_ge(pool_const, 2)
            for _ in range(18):
                nc.tensor.matmul(bank[6][:, 0:P], ones[:, :], ones[:, :], start=True, stop=True)
            pe.wait_ge(const_loaded, 16)
            for s in plan:
                kind, a = s[0], s[1:]
                if kind == "ln_cols":
                    pe.wait_ge(ln_loaded, 16)
                    wait_bank(pe, s)
                    nc.tensor.transpose(at_bank(s)[:, 0:KT], ln_rows[:, :], ident[0:KT, 0:KT]).then_inc(full(s), 1)
                elif kind == "cols":
                    pe.wait_ge(rows_loaded, 16 * 5)
                    wait_bank(pe, s)
                    nc.tensor.transpose(at_bank(s)[:, 0:ROWS], rows[:, :], ident[0:ROWS, 0:ROWS]).then_inc(full(s), 1)
                elif kind == "x":
                    t = a[0]
                    pe.wait_ge(x_normed, t + 1)
                    for k in range(KT):
                        key = ("xT", k)
                        if t == 0:
                            wait_bank(pe, key)
                        ins = nc.tensor.transpose(at_bank(key)[:, t * P:(t + 1) * P], x_sb[:, t, k * P:(k + 1) * P],
                                                  ident)
                        if t == NT - 1:
                            ins.then_inc(full(key), 1)
                elif kind == "main":
                    main(a[0])
                elif kind == "miscT":
                    wait_out(pe, ("misc", 0))
                    wait_bank(pe, s)
                    for t in range(NT):
                        ins = nc.tensor.transpose(at_bank(s)[:, t * MISC:(t + 1) * MISC],
                                                  miscT[:, t * P:(t + 1) * P], ident[0:MISC, 0:MISC])
                    ins.then_inc(full(s), 1)
                elif kind == "kiT":
                    pe.wait_ge(ik_ready, 2)
                    transposes(s, [ik_n[:, t, :] for t in range(NT)])
                elif kind == "gcum":
                    pe.wait_ge(g_ready, 1)
                    pe.wait_ge(pool_const, 2)
                    wait_bank(pe, s)
                    g16 = g.rearrange("p t h -> p (t h)")
                    nc.tensor.matmul(at_bank(s)[:, 0:16], tri, g16, start=True, stop=True)
                    nc.tensor.matmul(at_bank(s)[:, 16:32], ones[:, :], g16, start=True, stop=True).then_inc(full(s), 1)
                elif kind == "idx":
                    qb, h = a
                    wait_out(pe, ("iq", h // 2))
                    if nth[s] == 0:
                        wait_out(pe, ("kiT",))
                    wait_bank(pe, s)
                    r = slice((h % 2) * AD, (h % 2) * AD + AD)
                    n = (qb + 1) * P
                    nc.tensor.matmul(at_bank(s)[:, 0:n], iqT[r, h // 2, (qb - 1) * P:qb * P], kiT[r, 0:n],
                                     start=True, stop=True).then_inc(full(s), 1)
                elif kind in ("kT", "qT"):
                    if a[0] == 0:
                        pe.wait_ge(qk_normed, NT if kind == "kT" else 2 * NT)
                    transposes(s, [qk_raw[:, t, a[0] * P:(a[0] + 1) * P] for t in range(NT)])
                elif kind == "qk":
                    qb, h = divmod(a[0], AH)
                    wait_out(pe, ("qT", h // 2))
                    wait_out(pe, ("kT", h // 2))
                    wait_bank(pe, s)
                    r = slice((h % 2) * AD, (h % 2) * AD + AD)
                    n = (qb + 1) * P
                    nc.tensor.matmul(at_bank(s)[:, 0:n], qT[r, h // 2, qb * P:(qb + 1) * P], kT[r, h // 2, 0:n],
                                     start=True, stop=True).then_inc(full(s), 1)
                elif kind == "pt":
                    i = a[0]
                    pe.wait_ge(prob_normed, i + 1)
                    transposes(s, [prob[:, i % 3, j * P:(j + 1) * P] for j in range(i // AH + 1)])
                elif kind == "av":
                    i = a[0]
                    qb, h = divmod(i, AH)
                    if h == 0:
                        wait_bank(pe, ("O", qb))
                        wait_out(pe, ("av", qb))
                    wait_out(pe, ("pt", i))
                    dst = bank[7][(h % 2) * AD:(h % 2) * AD + AD, (h // 2) * P:(h // 2 + 1) * P]
                    for j in range(qb + 1):
                        ins = nc.tensor.matmul(dst, v_sb[:, j, h * AD:(h + 1) * AD], probT[:, i % 2, j * P:(j + 1) * P],
                                               start=(j == 0), stop=(j == qb))
                    ins.then_inc(full(("O", qb)) if h == AH - 1 else av_done, 1)
                elif kind == "dA":
                    c = a[0]
                    for n, x_ in enumerate("kq"):
                        pe.wait_ge(conv_silu, 4 * (n + 1))
                        transposes((x_, c), [conv_out[:, 4 * n + h, c * P:(c + 1) * P] for h in range(DH)])
                elif kind == "dV":
                    c = a[0]
                    pe.wait_ge(conv_silu, 12)
                    transposes(("v", c), [conv_out[:, 8 + h, c * P:(c + 1) * P] for h in range(DH)])
                elif kind == "dB":
                    c = a[0]
                    wait_out(pe, ("k", c))
                    transposes(("knT", c), [k_n[:, c % 2, h, :] for h in range(DH)])
                    wait_out(pe, ("q", c))
                    transposes(("qnT", c), [q_n[:, c % 2, h, :] for h in range(DH)])
                elif kind == "dE":
                    c = a[0]
                    pe.wait_ge(d_scaled, 3 * c + 3)
                    transposes(("qeT", c), [q_e[:, h, :] for h in range(DH)])
                elif kind == "dec":
                    c = a[0]
                    if c == 0:
                        pe.wait_ge(masks_cast, 2)
                    wait_bank(pe, s)
                    nc.tensor.matmul(heads(at_bank(s)[:, :]), ident_bf, keep_lower.unsqueeze(1).to_broadcast([P, DH, P]),
                                     start=True, stop=False, skip_group_check=True)
                    for h in range(DH):
                        ins = nc.tensor.matmul(at_bank(s)[:, h * P:(h + 1) * P], g[:, c, h:h + 1].to_broadcast([P, P]),
                                               tri, start=False, stop=(h == DH - 1), skip_group_check=True)
                    ins.then_inc(full(s), 1)
                elif kind == "decT":
                    wait_out(pe, ("dec", a[0]))
                    transposes(s, [a_neg[:, a[0], h, :] for h in range(DH)])
                elif kind == "dC":
                    c = a[0]
                    wait_out(pe, ("knT", c))
                    wait_out(pe, ("qnT", c))
                    for b in range(2):
                        key = ("kk", c, b)
                        wait_bank(pe, key)
                        for i in range(2):
                            h = 2 * b + i
                            ins = nc.tensor.matmul(at_bank(key)[:, i * 256:(i + 1) * 256], kqT[:, h, 0, :],
                                                   kqT[:, h, :, :].rearrange("p x n -> p (x n)"), start=True, stop=True)
                        ins.then_inc(full(key), 1)
                elif kind == "Z":
                    c, l = a
                    if l == 0:
                        pe.wait_ge(kk_done, 2 * c + 2)
                        transposes(s, [a_neg[:, c, h, :] for h in range(DH)])
                    else:
                        if l > 1:
                            wait_out(pe, ("U", c, l - 1))
                        wait_bank(pe, s)
                        for h in range(DH):
                            if l >= MASKED:
                                for up, low in blocks(l):
                                    ins = nc.tensor.matmul(at_bank(s)[up, h << l:(h + 1) << l], a_neg[low, c, h, up],
                                                           inv_u[low, c % 2, h, low], start=True, stop=True)
                                continue
                            u_h = heads(zc[:, c % 2, 0, :])[:, h, :] if l == 1 else inv_u[:, c % 2, h, :]
                            ins = nc.tensor.matmul(at_bank(s)[:, h * P:(h + 1) * P], a_neg[:, c, h, :], u_h,
                                                   start=True, stop=True)
                        ins.then_inc(full(s), 1)
                elif kind == "TU":
                    c, l = a
                    z = heads(zc[:, c % 2, l, :])
                    wait_out(pe, ("Z", c, l))
                    if l:
                        wait_t(pe, c, l - 1)
                        for x_ in ("T", "U"):
                            key = (x_, c, l)
                            if key not in use:
                                continue
                            wait_bank(pe, key)
                            for h in range(DH):
                                lhs, rhs = z[:, h, :], inv_t[:, c % 2, h, :]
                                if x_ == "U":
                                    lhs, rhs = rhs, lhs
                                if l < MASKED:
                                    ins = nc.tensor.matmul(at_bank(key)[:, h * P:(h + 1) * P], lhs, rhs, start=True,
                                                           stop=True)
                                    continue
                                for up, low in blocks(l):
                                    z_b, t_b = zc[up, c % 2, l, h << l:(h + 1) << l], inv_t[up, c % 2, h, up]
                                    dst = at_bank(key)[up if x_ == "U" else low, h << l:(h + 1) << l]
                                    if x_ == "U":
                                        ins = nc.tensor.matmul(dst, t_b, z_b, start=True, stop=True)
                                    elif up.start == 0:
                                        ins = nc.tensor.matmul(dst, z_b, t_b, start=True, stop=True)
                            ins.then_inc(full(key), 1)
                elif kind == "uw":
                    c = a[0]
                    wait_out(pe, ("U", c, LEVELS - 1))
                    pe.wait_ge(d_scaled, 3 * c + 3)
                    for key in (("u", c), ("w", c)):
                        wait_bank(pe, key)
                        for h in range(DH):
                            u_h = inv_u[:, c % 2, h, :]
                            lhs, rhs = (u_h, v_b[:, c, h, :]) if key[0] == "u" else (k_bg[:, c, h, :], u_h)
                            ins = nc.tensor.matmul(at_bank(key)[:, h * P:(h + 1) * P], lhs, rhs, start=True, stop=True)
                        ins.then_inc(full(key), 1)
                elif kind == "ws" and a[0] > 0:
                    c = a[0]
                    wait_out(pe, ("w", c))
                    wait_out(pe, ("kv", c - 1))
                    wait_bank(pe, s)
                    for h in range(DH):
                        ins = nc.tensor.matmul(at_bank(s)[:, h * P:(h + 1) * P], k_bg[:, c, h, :], state[:, c % 2, h, :],
                                               start=True, stop=True)
                    ins.then_inc(full(s), 1)
                elif kind == "kv" and a[0] < NT - 1:
                    c = a[0]
                    wait_out(pe, ("ws", c) if c else ("u", 0))
                    wait_bank(pe, s)
                    for h in range(DH):
                        vn = v_new[:, c % 2, h, :] if c else v_b[:, 0, h, :]
                        ins = nc.tensor.matmul(at_bank(s)[:, h * P:(h + 1) * P], k_dec[:, c, h, :], vn, start=True,
                                               stop=True)
                    ins.then_inc(full(s), 1)
                elif kind == "o":
                    c = a[0]
                    if c == NT - 1:
                        wait_out(pe, ("ws", c))
                    wait_out(pe, ("qeT", c))
                    wait_bank(pe, s)
                    for h in range(DH):
                        dst = at_bank(s)[:, h * P:(h + 1) * P]
                        if c:
                            nc.tensor.matmul(dst, qeT[:, c, h, :], state[:, c % 2, h, :], start=True, stop=False)
                        vn = v_new[:, c % 2, h, :] if c else v_b[:, 0, h, :]
                        ins = nc.tensor.matmul(dst, intraT[:, c, h, :], vn, start=(c == 0), stop=True)
                    ins.then_inc(full(s), 1)
                elif kind == "mixT":
                    k = a[0]
                    if k == 4:
                        pe.wait_ge(delta_mixed, NT)
                    transposes(s, [gate[:, t, k * P:(k + 1) * P] for t in range(NT)])

        @block.scalar
        def _(act):
            own = [0]

            def link(ins):
                own[0] += 1
                ins.then_inc(act_own, 1)
                act.wait_ge(act_own, own[0])

            def split_hi(u):
                act.wait_ge(raw_loaded[u % RAW_RING], 16 * (u // RAW_RING + 1) + (16 if u % RAW_RING == 0 else 0))
                if u >= SPLIT_RING:
                    wait_unit_used(act, u - SPLIT_RING)
                n = unit_width(u)
                nc.scalar.activation(w_hi[:, u % SPLIT_RING, 0:n], w_raw[:, u % RAW_RING, 0:n], ACT.Copy).then_inc(
                    hi_ready, 1)

            def copy_out(key, dst, func=ACT.Copy, src=None, **kw):
                wait_full(act, key)
                nc.scalar.activation(dst, at_bank(key)[:, :] if src is None else src, func, **kw).then_inc(free(key), 1)

            for t in range(NT):
                act.wait_ge(x_loaded[t], 16)
                if t:
                    act.wait_ge(x_squared, t)
                nc.scalar.activation(junk, x_sb[:, t, :], ACT.Square, accum_out=ss_x[:, t:t + 1]).then_inc(x_squared, 1)
            for s in plan:
                kind, a = s[0], s[1:]
                if kind == "ln_cols":
                    copy_out(s, ln_cols[:, :], src=at_bank(s)[:, 0:KT])
                    split_hi(0)
                elif kind == "cols":
                    copy_out(s, cols[:, :], src=at_bank(s)[:, 0:ROWS])
                elif kind == "xT":
                    if a[0] == 0:
                        wait_out(act, ("ln_cols",))
                    wait_full(act, s)
                    nc.scalar.activation(in_hi[:, a[0], :], at_bank(s)[:, :], ACT.Copy,
                                         scale=ln_cols[:, a[0]:a[0] + 1]).then_inc(in_hi_ready, 1)
                    if a[0] == 3:
                        split_hi(1)
                elif kind == "main":
                    if a[0] + AHEAD < len(UNITS):
                        split_hi(a[0] + AHEAD)
                elif kind == "evac":
                    name = a[0]
                    for j in range(tiles(name)):
                        key = (name, j)
                        if name == "misc":
                            copy_out(key, miscT, src=at_bank(key)[0:MISC, :])
                        elif name == "iq":
                            if j == 0:
                                wait_full(act, ("kiT",))
                            copy_out(key, iqT[:, j, :], src=at_bank(key)[:, 0:SEQ - P])
                        elif name in ("ak", "aq"):
                            copy_out(key, qk_raw[:, j, :])
                        elif name == "av":
                            copy_out(key, v_sb[:, j, :])
                        elif name == "ag":
                            copy_out(key, gate[:, j, 0:GW], ACT.Silu)
                        elif name == "dz":
                            copy_out(key, gate[:, j, GW:D], ACT.Silu)
                        elif name in ("dk", "dq", "dv"):
                            n = ("dk", "dq", "dv").index(name)
                            if n:
                                act.wait_ge(conv_done, 4 * (n - 1) + j + 1)
                            copy_out(key, conv_in[:, j, 3:])
                elif kind == "miscT":
                    copy_out(s, misc[:, :, :].rearrange("p t n -> p (t n)"), src=at_bank(s)[:, 0:NT * MISC])
                elif kind == "gates":
                    act.wait_ge(gate_in, 1)
                    link(nc.scalar.activation(e_nab, nab, ACT.Exp))
                    nc.scalar.activation(ln_sp, e_nab, ACT.Ln, bias=1.0).then_inc(gate_exp, 1)
                    nc.scalar.activation(e_b, misc[:, :, 72:76], ACT.Exp, scale=-1.0).then_inc(gate_exp, 1)
                    act.wait_ge(par_loaded, 16 * 3)
                    nc.scalar.activation(exp_alog, alog_bc, ACT.Exp).then_inc(gate_exp, 1)
                elif kind == "gcum":
                    act.wait_ge(gcum_ready, 1)
                    nc.scalar.activation(e_g, gc, ACT.Exp).then_inc(gcum_exp, 1)
                    nc.scalar.activation(e_last, g_last, ACT.Exp).then_inc(gcum_exp, 1)
                    nc.scalar.activation(e_diff, diff, ACT.Exp).then_inc(gcum_exp, 1)
                elif kind == "idx":
                    n = (a[0] + 1) * P
                    if nth[s] >= 2:
                        act.wait_ge(idx_added, nth[s] - 1)
                    copy_out(s, relu[:, nth[s] % 2, 0:n], ACT.Relu, src=at_bank(s)[:, 0:n])
                elif kind == "norm":
                    for t in range(NT):
                        n = nth[s] * NT + t
                        wait_out(act, (a[0], t))
                        if n >= 2:
                            act.wait_ge(qk_summed, n - 1)
                        nc.scalar.activation(masked[:, n % 2, :], qk_raw[:, t, :], ACT.Square).then_inc(qk_squared, 1)
                elif kind in ("kT", "qT"):
                    c = R_WK if kind == "kT" else R_WQ
                    copy_out(s, (kT if kind == "kT" else qT)[:, a[0], :], scale=cols[:, c:c + 1])
                elif kind == "qk":
                    i = a[0]
                    n = (i // AH + 1) * P
                    act.wait_ge(nmx_ready, i + 1)
                    if i >= 3:
                        wait_full(act, ("pt", i - 3))
                    nc.scalar.activation(prob[:, i % 3, 0:n], masked[:, i % 2, 0:n], ACT.Exp, bias=nmx[:, i:i + 1],
                                         scale=AD ** -0.5, accum_out=p_sum[:, i:i + 1]).then_inc(exp_done, 1)
                elif kind == "pt":
                    i = a[0]
                    n = (i // AH + 1) * P
                    if i % 2 == 0:
                        if i >= 2:
                            wait_av(act, i - 2)
                        copy_out(s, probT[:, i % 2, 0:n], src=at_bank(s)[:, 0:n])
                elif kind == "silu":
                    n = ("dk", "dq", "dv").index(a[0])
                    for j in range(4):
                        act.wait_ge(conv_done, 4 * n + j + 1)
                        y = conv_out[:, 4 * n + j, :]
                        nc.scalar.activation(y, y, ACT.Silu).then_inc(conv_silu, 1)
                elif kind == "dA":
                    c = a[0]
                    for i, x_ in enumerate("kq"):
                        wait_full(act, (x_, c))
                        if c or i:
                            act.wait_ge(d_summed, 2 * c + i)
                        nc.scalar.activation(sq, at_bank((x_, c))[:, :], ACT.Square).then_inc(d_squared, 1)
                elif kind == "dV" and a[0] % 2 == 0:
                    c = a[0]
                    wait_full(act, ("v", c))
                    for h in range(DH):
                        ins = nc.scalar.activation(v_b[:, c, h, :], at_bank(("v", c))[:, h * P:(h + 1) * P], ACT.Copy,
                                                   scale=beta[:, c, h:h + 1])
                    ins.then_inc(free(("v", c)), 1)
                elif kind == "dB":
                    c = a[0]
                    if c:
                        wait_full(act, ("kk", c - 1, 1))
                    copy_out(("knT", c), kqT[:, :, 0, :], src=heads(at_bank(("knT", c))[:, :]))
                    copy_out(("qnT", c), kqT[:, :, 1, :], src=heads(at_bank(("qnT", c))[:, :]))
                elif kind == "dE":
                    c = a[0]
                    copy_out(("qeT", c), qeT[:, c, :, :], src=heads(at_bank(("qeT", c))[:, :]))
                elif kind == "dec":
                    c = a[0]
                    act.wait_ge(gcum_done, 1)
                    wait_out(act, ("O", NT - 1))
                    wait_full(act, s)
                    for h in range(DH):
                        ins = nc.scalar.activation(a_neg[:, c, h, :], at_bank(s)[:, h * P:(h + 1) * P], ACT.Exp,
                                                   bias=gc[:, c * DH + h:c * DH + h + 1], scale=-1.0)
                    ins.then_inc(free(s), 1)
                elif kind == "decT":
                    copy_out(s, intraT[:, a[0], :, :], src=heads(at_bank(s)[:, :]))
                elif kind == "ones":
                    for x_ in "kqv":
                        wait_full(act, (x_, NT - 1))
                    nc.scalar.activation(heads(zc[:, 1, a[0], :]), ident.unsqueeze(1).to_broadcast([P, DH, P]),
                                         ACT.Copy).then_inc(zc_ones_a, 1)
                elif kind == "TU":
                    c, l = a
                    keys = [k for k in (("T", c, l), ("U", c, l)) if k in use]
                    for key in keys:
                        wait_full(act, key)
                    for key in keys:
                        if l < MASKED:
                            copy_out(key, inv_u[:, c % 2, :, :], src=heads(at_bank(key)[:, :]))
                        elif key[0] == "T":
                            up, low = blocks(l)[0]
                            copy_out(key, inv_t[low, c % 2, :, up], src=heads(at_bank(key)[low, 0:DH << l]))
                        else:
                            for up, low in blocks(l):
                                ins = nc.scalar.activation(inv_u[up, c % 2, :, low], heads(at_bank(key)[up, 0:DH << l]),
                                                           ACT.Copy)
                            ins.then_inc(free(key), 1)
                elif kind == "uw":
                    copy_out(("u", a[0]), v_b[:, a[0], :, :], src=heads(at_bank(("u", a[0]))[:, :]))
                    copy_out(("w", a[0]), k_bg[:, a[0], :, :], src=heads(at_bank(("w", a[0]))[:, :]))
                elif kind == "onorm":
                    c = a[0]
                    wait_full(act, ("o", c))
                    wait_full(act, ("kk", NT - 1, 1))
                    if c:
                        wait_out(act, ("o", c - 1))
                    for h in range(DH):
                        ins = nc.scalar.activation(o_sq, at_bank(("o", c))[:, h * P:(h + 1) * P], ACT.Square,
                                                   accum_out=ss_o[:, h:h + 1])
                        if h < DH - 1:
                            link(ins)
                    ins.then_inc(o_squared, 1)
                elif kind == "mixC":
                    if a[0] == 0:
                        wait_out(act, ("O", NT - 1))
                        for j in range(4):
                            wait_full(act, ("dz", j))
                    nc.scalar.activation(in_hi[:, a[0], :], gate[:, a[0], 0:GW], ACT.Copy).then_inc(mix_hi_ready, 1)
                elif kind == "mixT":
                    wait_full(act, s)
                    nc.scalar.activation(in_hi[:, a[0], :], at_bank(s)[:, :], ACT.Copy).then_inc(in_hi_ready, 1)

        @block.vector
        def _(dve):
            own = [0]

            def link(ins):
                own[0] += 1
                ins.then_inc(vec, 1)
                dve.wait_ge(vec, own[0])

            def variance(key, src, scale):
                lo, hi = norm_at[key]
                nc.vector.tensor_scalar(var[:, lo:hi], src, scale, EPS, ALU.mult, ALU.add).then_inc(var_ready, 1)

            def root(key):
                lo, hi = norm_at[key]
                dve.wait_ge(rstd_ready, norm_no[key] + 1)
                return rstd[:, lo:hi]

            variance_x = [0]
            for t in range(NT + 1):
                if t < NT:
                    dve.wait_ge(x_squared, t + 1)
                    variance(("x", t), ss_x[:, t:t + 1], 1.0 / D)
                if t:
                    r = root(("x", t - 1))
                    nc.vector.tensor_scalar(x_sb[:, t - 1, :], x_sb[:, t - 1, :], r, None, ALU.mult).then_inc(
                        x_normed, 1)
            for s in plan:
                kind, a = s[0], s[1:]
                if kind in ("xT", "mixT"):
                    k = a[0]
                    dve.wait_ge(in_hi_ready, nth[s] + 1 + (KT if kind == "mixT" else 0))
                    hi = in_hi[:, k, :].bitcast(F32)
                    if kind == "xT":
                        wait_out(dve, ("ln_cols",))
                        ins = nc.vector.scalar_tensor_tensor(in_lo[:, k, :], at_bank(s)[:, :],
                                                             ln_cols[:, k:k + 1], hi, ALU.mult, ALU.subtract)
                    else:
                        ins = nc.vector.tensor_tensor(in_lo[:, k, :], at_bank(s)[:, :], hi, ALU.subtract)
                    ins.then_inc(free(s), 1)
                elif kind == "gates":
                    wait_out(dve, ("miscT",))
                    dve.wait_ge(par_loaded, 16 * 3)
                    link(nc.vector.tensor_tensor(y_dt, misc[:, :, 76:80], dt_bc.unsqueeze(1).to_broadcast([P, NT, DH]),
                                                 ALU.add))
                    nc.vector.scalar_tensor_tensor(nab, y_dt, -1.0, y_dt, ALU.mult, ALU.min).then_inc(gate_in, 1)
                    ik = misc[:, :, 0:AD]
                    link(nc.vector.tensor_reduce(mu_s, ik, AX.X, ALU.add))
                    link(nc.vector.tensor_scalar(mu, mu_s, 1.0 / AD, None, ALU.mult))
                    link(nc.vector.tensor_tensor(ik_c, ik, over(mu, AD), ALU.subtract))
                    link(nc.vector.tensor_tensor(ik_sq, ik_c, ik_c, ALU.mult))
                    link(nc.vector.tensor_reduce(ss_ik, ik_sq, AX.X, ALU.add))
                    variance(("ik",), ss_ik, 1.0 / AD)
                    nc.vector.tensor_scalar(w_i, misc[:, :, 64:72], AH ** -0.5 * AD ** -0.5, None, ALU.mult)
                    dve.wait_ge(gate_exp, 3)
                    link(nc.vector.tensor_scalar(beta, e_b, 1.0, None, ALU.add))
                    link(nc.vector.reciprocal(beta, beta))
                    nc.vector.tensor_scalar(nbeta, beta, -1.0, None, ALU.mult)
                    link(nc.vector.scalar_tensor_tensor(soft, y_dt, 0.0, ln_sp, ALU.max, ALU.add))
                    nc.vector.scalar_tensor_tensor(g, soft, -1.0, exp_alog.unsqueeze(1).to_broadcast([P, NT, DH]),
                                                   ALU.mult, ALU.mult).then_inc(g_ready, 1)
                    r = root(("ik",))
                    for i in range(2):
                        nc.vector.tensor_tensor(ik_n[:, :, i * AD:(i + 1) * AD], ik_c, over(r, AD), ALU.mult).then_inc(
                            ik_ready, 1)
                elif kind == "kiT":
                    wait_out(dve, ("cols",))
                    dve.wait_ge(masks_loaded, 16)
                    nc.vector.tensor_copy(level_mask[:, :, :].rearrange("p l n -> p (l n)"),
                                          mask_words[:, 0:MASKED * P]).then_inc(masks_cast, 1)
                    nc.vector.tensor_copy(cbf[:, :], mask_words[:, MASKED * P:]).then_inc(masks_cast, 1)
                    wait_full(dve, s)
                    nc.vector.tensor_scalar(kiT, at_bank(s)[:, :], cols[:, R_IW:R_IW + 1], cols[:, R_IB:R_IB + 1],
                                            ALU.mult, ALU.add).then_inc(free(s), 1)
                elif kind == "gcum":
                    wait_full(dve, s)
                    nc.vector.tensor_copy(gc2, at_bank(s)[:, 0:32]).then_inc(free(s), 1)
                    wait_out(dve, s)
                    nc.vector.tensor_tensor(diff, g_last, gc, ALU.subtract).then_inc(gcum_ready, 1)
                    dve.wait_ge(gcum_exp, 3)
                    nc.vector.tensor_tensor(b_eg, beta.rearrange("p t h -> p (t h)"), e_g, ALU.mult).then_inc(
                        gcum_done, 1)
                elif kind == "idx":
                    qb, h = a
                    n = (qb + 1) * P
                    wait_out(dve, s)
                    r, w = relu[:, nth[s] % 2, 0:n], w_i[:, qb, h:h + 1]
                    if h == 0:
                        ins = nc.vector.tensor_scalar(score[:, qb, 0:n], r, w, None, ALU.mult)
                    else:
                        dve.wait_ge(idx_added, nth[s])
                        ins = nc.vector.scalar_tensor_tensor(score[:, qb, 0:n], r, w, score[:, qb, 0:n], ALU.mult,
                                                             ALU.add)
                    ins.then_inc(idx_added, 1)
                elif kind == "topk":
                    qb, part_, parts = a
                    sc = score[:, qb, 0:(qb + 1) * P]
                    if part_ == 0:
                        dve.wait_ge(causal_done, qb)
                    for _ in range(TOPK // 8 // parts):
                        link(nc.vector.max(top8, sc))
                        link(nc.vector.match_replace(sc, top8, sc, TAKEN))
                    if part_ == parts - 1:
                        nc.vector.tensor_scalar(sc, sc, 0.97 * TAKEN, NEG, ALU.is_gt, ALU.mult).then_inc(kept_ready, 1)
                elif kind == "norm":
                    for t in range(NT):
                        n = nth[s] * NT + t
                        dve.wait_ge(qk_squared, n + 1)
                        nc.vector.tensor_reduce(ss_att[:, t, :], masked[:, n % 2, :].rearrange(
                            "p (h d) -> p h d", h=AH), AX.X, ALU.add).then_inc(qk_summed, 1)
                    dve.wait_ge(qk_summed, (nth[s] + 1) * NT)
                    variance((a[0],), ss_att.rearrange("p t h -> p (t h)"), 1.0 / AD)
                elif kind == "scale":
                    r = root((a[0],))
                    raw_heads = [qk_raw[:, t, :].rearrange("p (h d) -> p h d", h=AH) for t in range(NT)]
                    for t in range(NT):
                        nc.vector.tensor_tensor(raw_heads[t], raw_heads[t], over(r[:, t * AH:(t + 1) * AH], AD),
                                                ALU.mult).then_inc(qk_normed, 1)
                elif kind == "qk":
                    i = a[0]
                    qb = i // AH
                    n = (qb + 1) * P
                    wait_full(dve, s)
                    if i >= 2:
                        dve.wait_ge(exp_done, i - 1)
                    if i == 0:
                        dve.wait_ge(pool_const, 5)
                    else:
                        dve.wait_ge(kept_ready, qb) if qb else None
                    nc.vector.tensor_tensor_reduce(masked[:, i % 2, 0:n], at_bank(s)[:, 0:n], score[:, qb, 0:n], 1.0,
                                                   TAKEN, ALU.add, ALU.max, mx[:, i:i + 1]).then_inc(free(s), 1)
                    wait_out(dve, s)
                    nc.vector.tensor_scalar(nmx[:, i:i + 1], mx[:, i:i + 1], -AD ** -0.5, None, ALU.mult).then_inc(
                        nmx_ready, 1)
                elif kind == "pt":
                    i = a[0]
                    n = (i // AH + 1) * P
                    if i % 2:
                        if i >= 2:
                            wait_av(dve, i - 2)
                        wait_full(dve, s)
                        nc.vector.tensor_copy(probT[:, i % 2, 0:n], at_bank(s)[:, 0:n]).then_inc(free(s), 1)
                elif kind == "omix":
                    qb = a[0]
                    wait_full(dve, ("O", qb))
                    for j in range(4):
                        wait_out(dve, ("ag", j))
                    y = gate[:, :, qb * P:(qb + 1) * P]
                    nc.vector.tensor_tensor(y, heads(bank[7][:, :]), y, ALU.mult).then_inc(free(("O", qb)), 1)
                elif kind == "pn":
                    i = a[0]
                    dve.wait_ge(exp_done, i + 1)
                    nc.vector.reciprocal(p_sum[:, i:i + 1], p_sum[:, i:i + 1]).then_inc(r_ready, 1)
                elif kind == "conv":
                    name, j = a
                    n = ("dk", "dq", "dv").index(name)
                    wait_out(dve, (name, j))
                    if n == 0 and j == 0:
                        dve.wait_ge(pool_const, 3)
                    y = conv_out[:, 4 * n + j, :]
                    tile = ("dq", "dk", "dv").index(name) * 4 + j

                    def tap(i):
                        c = R_CONV + 12 * i + tile
                        return cols[:, c:c + 1]

                    link(nc.vector.tensor_scalar(y, conv_in[:, j, 0:SEQ], tap(0), None, ALU.mult))
                    for i in range(1, TAPS):
                        ins = nc.vector.scalar_tensor_tensor(y, conv_in[:, j, i:i + SEQ], tap(i), y, ALU.mult, ALU.add)
                        if i < TAPS - 1:
                            link(ins)
                    ins.then_inc(conv_done, 1)
                elif kind == "dA":
                    c = a[0]
                    if c:
                        dve.wait_ge(var_ready, norm_no[("dqk", c - 1)] + 1)
                    for i, x_ in enumerate("kq"):
                        dve.wait_ge(d_squared, 2 * c + i + 1)
                        nc.vector.tensor_reduce(ss_d[:, i * DH:(i + 1) * DH], heads(sq), AX.X, ALU.add).then_inc(
                            d_summed, 1)
                    dve.wait_ge(d_summed, 2 * c + 2)
                    variance(("dqk", c), ss_d, 1.0)
                elif kind == "dV" and a[0] % 2:
                    c = a[0]
                    wait_full(dve, ("v", c))
                    nc.vector.tensor_tensor(v_b[:, c, :, :], heads(at_bank(("v", c))[:, :]), over(beta[:, c, :], DD),
                                            ALU.mult).then_inc(free(("v", c)), 1)
                elif kind == "dS":
                    c = a[0]
                    r = root(("dqk", c))
                    if c > 1:
                        wait_full(dve, ("qnT", c - 2))
                        dve.wait_ge(d_scaled, 3 * (c - 1))
                    nc.vector.tensor_tensor(k_n[:, c % 2, :, :], heads(at_bank(("k", c))[:, :]), over(r[:, 0:DH], DD),
                                            ALU.mult).then_inc(free(("k", c)), 1)
                    if c:
                        wait_out(dve, ("q", c - 1))
                    link(nc.vector.tensor_scalar(r_q, r[:, DH:2 * DH], DD ** -0.5, None, ALU.mult))
                    nc.vector.tensor_tensor(q_n[:, c % 2, :, :], heads(at_bank(("q", c))[:, :]), over(r_q, DD),
                                            ALU.mult).then_inc(free(("q", c)), 1)
                elif kind == "dC":
                    c = a[0]
                    wait_out(dve, ("decT", c))
                    for b in range(2):
                        key = ("kk", c, b)
                        wait_full(dve, key)
                        src = at_bank(key)[:, :].rearrange("p (h x n) -> p h x n", h=2, x=2)
                        for i in range(2):
                            h = 2 * b + i
                            ins = nc.vector.scalar_tensor_tensor(a_neg[:, c, h, :], src[:, i, 0, :], nbeta[:, c, h:h + 1],
                                                           a_neg[:, c, h, :], ALU.mult, ALU.mult)
                        ins.then_inc(kk_done, 1)
                        nc.vector.tensor_tensor(intraT[:, c, 2 * b:2 * b + 2, :], src[:, :, 1, :],
                                                intraT[:, c, 2 * b:2 * b + 2, :], ALU.mult).then_inc(free(key), 1)
                elif kind == "ones":
                    for x_ in "kqv":
                        wait_full(dve, (x_, NT - 1))
                    nc.vector.tensor_copy(heads(zc[:, 0, a[0], :]),
                                          ident.unsqueeze(1).to_broadcast([P, DH, P])).then_inc(zc_ones_v, 1)
                elif kind == "Z":
                    c, l = a
                    wait_full(dve, s)
                    if l >= MASKED:
                        for up, low in blocks(l):
                            ins = nc.vector.tensor_copy(zc[up, c % 2, l, 0:DH << l], at_bank(s)[up, 0:DH << l])
                        ins.then_inc(free(s), 1)
                        continue
                    dve.wait_ge(zc_ones_a if c % 2 else zc_ones_v, l + 1)
                    dve.wait_ge(masks_cast, 1)
                    nc.vector.copy_predicated(heads(zc[:, c % 2, l, :]),
                                              level_mask[:, l, :].unsqueeze(1).to_broadcast([P, DH, P]),
                                              heads(at_bank(s)[:, :])).then_inc(free(s), 1)
                elif kind == "TU" and a[1] < LEVELS - 2:
                    c, l = a
                    if l:
                        wait_out(dve, ("U", c, l))
                    else:
                        wait_out(dve, ("Z", c, 0))
                        if c > 1:
                            wait_full(dve, ("U", c - 2, LEVELS - 1))
                    src = inv_u[:, c % 2, :, :].rearrange("p h n -> p (h n)") if l else zc[:, c % 2, 0, :]
                    nc.vector.transpose(inv_t[:, c % 2, :, :].rearrange("p h n -> p (h n)"), src).then_inc(t_ready, 1)
                elif kind == "ws" and a[0] > 0:
                    c = a[0]
                    wait_full(dve, s)
                    wait_out(dve, ("u", c))
                    nc.vector.tensor_tensor(v_new[:, c % 2, :, :], v_b[:, c, :, :], heads(at_bank(s)[:, :]),
                                            ALU.subtract).then_inc(free(s), 1)
                elif kind == "kv" and a[0] < NT - 1:
                    c = a[0]
                    wait_full(dve, s)
                    if c == 0:
                        nc.vector.tensor_copy(state[:, 1, :, :], heads(at_bank(s)[:, :])).then_inc(free(s), 1)
                    else:
                        wait_out(dve, ("kv", c - 1))
                        for h in range(DH):
                            ins = nc.vector.scalar_tensor_tensor(
                                state[:, (c + 1) % 2, h, :], state[:, c % 2, h, :],
                                e_last[:, c * DH + h:c * DH + h + 1], at_bank(s)[:, h * P:(h + 1) * P], ALU.mult, ALU.add)
                        ins.then_inc(free(s), 1)
                elif kind == "onorm":
                    c = a[0]
                    dve.wait_ge(o_squared, c + 1)
                    variance(s, ss_o, 1.0 / DD)
                elif kind == "oscale":
                    c = a[0]
                    r = root(("onorm", c))
                    if c:
                        dve.wait_ge(delta_mixed, c)
                    nc.vector.tensor_tensor(heads(o_tmp), heads(at_bank(("o", c))[:, :]), over(r, DD),
                                            ALU.mult).then_inc(free(("o", c)), 1)
                    if c == NT - 1:
                        wait_out(dve, ("o", c))
                        dve.wait_ge(dz_scaled, c + 1)
                        nc.vector.tensor_tensor(gate[:, c, GW:D], o_tmp, gate[:, c, GW:D], ALU.mult).then_inc(
                            delta_mixed, 1)
                elif kind == "evac" and a[0][:3] == "out":
                    n = int(a[0][3])
                    if n == 0:
                        dve.wait_ge(x_again, 16 * NT)
                    for j in range(4):
                        key = (a[0], j)
                        wait_full(dve, key)
                        y = x_sb[:, j, n * GW:(n + 1) * GW]
                        nc.vector.tensor_tensor(y, at_bank(key)[:, :], y, ALU.add).then_inc(free(key), 1)

        @block.gpsimd
        def _(pool):
            def split_lo(u):
                pool.wait_ge(hi_ready, u + 1)
                if u >= SPLIT_RING:
                    wait_unit_used(pool, u - SPLIT_RING)
                n = unit_width(u)
                nc.gpsimd.tensor_tensor(w_lo[:, u % SPLIT_RING, 0:n], w_raw[:, u % RAW_RING, 0:n],
                                        w_hi[:, u % SPLIT_RING, 0:n].bitcast(F32), ALU.subtract).then_inc(lo_ready, 1)

            def power(key):
                lo, hi = norm_at[key]
                pool.wait_ge(var_ready, norm_no[key] + 1)
                nc.gpsimd.tensor_tensor(rstd[:, lo:hi], var[:, lo:hi], half[:, 0:hi - lo], ALU.pow).then_inc(
                    rstd_ready, 1)

            nc.gpsimd.memset(half[:, :], -0.5).then_inc(pool_const, 1)
            nc.gpsimd.memset(ones[:, :], 1.0).then_inc(pool_const, 1)
            nc.gpsimd.memset(conv_in[:, :, 0:TAPS - 1], 0.0).then_inc(pool_const, 1)
            first = score[:, 0, 0:P]
            nc.gpsimd.memset(first, 0.0).then_inc(pool_const, 1)
            pool.wait_ge(pool_const, 4)
            nc.gpsimd.affine_select(out=first, in_=first, compare_op=ALU.is_ge, fill=NEG, base=0, pattern=[[-1, P]],
                                    channel_multiplier=1).then_inc(pool_const, 1)
            for t in range(NT):
                power(("x", t))
            split_lo(0)
            split_lo(1)
            for s in plan:
                kind, a = s[0], s[1:]
                if kind == "main":
                    if a[0] + AHEAD < len(UNITS):
                        split_lo(a[0] + AHEAD)
                elif kind == "gates":
                    power(("ik",))
                elif kind == "causal":
                    qb = a[0]
                    d = score[:, qb, qb * P:(qb + 1) * P]
                    pool.wait_ge(idx_added, qb * AH)
                    nc.gpsimd.affine_select(out=d, in_=d, compare_op=ALU.is_ge, fill=NEG, base=0, pattern=[[-1, P]],
                                            channel_multiplier=1).then_inc(causal_done, 1)
                elif kind == "root":
                    power((a[0],))
                elif kind == "dA":
                    c = a[0]
                    power(("dqk", c))
                elif kind == "dS":
                    c = a[0]
                    sl = slice(c * DH, (c + 1) * DH)
                    if c == 0:
                        pool.wait_ge(gcum_done, 1)
                    wait_out(pool, ("k", c))
                    nc.gpsimd.tensor_tensor(k_bg[:, c, :, :], k_n[:, c % 2, :, :], over(b_eg[:, sl], DD),
                                            ALU.mult).then_inc(d_scaled, 1)
                    nc.gpsimd.tensor_tensor(k_dec[:, c, :, :], k_n[:, c % 2, :, :], over(e_diff[:, sl], DD),
                                            ALU.mult).then_inc(d_scaled, 1)
                    wait_out(pool, ("q", c))
                    if c:
                        wait_full(pool, ("qeT", c - 1))
                    nc.gpsimd.tensor_tensor(q_e, q_n[:, c % 2, :, :], over(e_g[:, sl], DD), ALU.mult).then_inc(
                        d_scaled, 1)
                elif kind == "dzw":
                    j = a[0]
                    wait_out(pool, ("dz", j))
                    y = heads(gate[:, j, GW:D])
                    nc.gpsimd.tensor_tensor(y, y, dnw[:, :].unsqueeze(1).to_broadcast([P, DH, DD]),
                                            ALU.mult).then_inc(dz_scaled, 1)
                elif kind == "pn":
                    i = a[0]
                    p = prob[:, i % 3, 0:(i // AH + 1) * P]
                    pool.wait_ge(r_ready, i + 1)
                    nc.gpsimd.tensor_scalar(p, p, p_sum[:, i:i + 1], None, ALU.mult).then_inc(prob_normed, 1)
                elif kind == "mixC":
                    k = a[0]
                    pool.wait_ge(mix_hi_ready, k + 1)
                    nc.gpsimd.tensor_tensor(in_lo[:, k, :], gate[:, k, 0:GW], in_hi[:, k, :].bitcast(F32),
                                            ALU.subtract).then_inc(mix_lo_ready, 1)
                elif kind == "onorm":
                    power(s)
                elif kind == "oscale" and a[0] < NT - 1:
                    c = a[0]
                    wait_out(pool, ("o", c))
                    pool.wait_ge(dz_scaled, c + 1)
                    nc.gpsimd.tensor_tensor(gate[:, c, GW:D], o_tmp, gate[:, c, GW:D], ALU.mult).then_inc(
                        delta_mixed, 1)


def constants():
    i = np.arange(P)
    row, col = i[:, None], i[None, :]
    levels = [((row >> (l + 1)) == (col >> (l + 1))) & ((row >> l) % 2 == 0) & ((col >> l) % 2 == 1)
              for l in range(MASKED)]
    lower = np.where(col <= row, 0.0, -NEG)
    return np.concatenate([row == col, row <= col, *levels, row == col, lower], axis=1).astype(np.float32)


_INS = ["x", "ln_w", "w_in", "attn_q_norm_w", "attn_k_norm_w", "idx_k_norm_w", "idx_k_norm_b", "dn_conv_w", "dn_A_log",
        "dn_dt_bias", "dn_norm_w", "w_out"]


def kernel(**inputs):
    import concourse.bacc as bacc
    from concourse.bass_utils import run_bass_kernel_spmd

    nc = bacc.Bacc("TRN2", target_bir_lowering=False, num_devices=1)
    arrays = {f"in_{n}": np.ascontiguousarray(inputs[n]) for n in _INS}
    arrays["constants"] = constants()
    args = [nc.dram_tensor(n, a.shape, mybir.dt.from_np(a.dtype), kind="ExternalInput").ap()
            for n, a in arrays.items()]
    out = nc.dram_tensor("out", (1, SEQ, D), F32, kind="ExternalOutput").ap()
    build(nc, *args, out)
    result = run_bass_kernel_spmd(nc, [arrays], core_ids=[0])
    return result.results[0]["out"]
```
